# Optimizing a Trainium2 kernel written in Bass

```python
import math
import jax, jax.numpy as jnp
from jax import lax
import numpy as np

D_MODEL = 2048
BATCH = 1
SEQ = 256
DEPTH = 1

GRID_W = 64
CTX_LEN = 256

GLA_HEADS = 4
GLA_DK = 128
GLA_DV = 256
GLA_KEY_WIDTH = GLA_HEADS * GLA_DK
GLA_VAL_WIDTH = GLA_HEADS * GLA_DV
GATE_RANK = 16
GATE_TAU = 16.0
CHUNK = 64

FOURIER_GROUPS = 4
FOURIER_GROUP_DIM = 256
FOURIER_WIDTH = FOURIER_GROUPS * FOURIER_GROUP_DIM

N_BRANCHES = 2
D_FF = 4 * D_MODEL
N_MOD = 6
EPS = 1e-6
POS_TEMP = 10000.0

IN_SPLIT_WIDTHS = (GLA_KEY_WIDTH, GLA_KEY_WIDTH, GLA_VAL_WIDTH, GLA_VAL_WIDTH,
                   GATE_RANK, GATE_RANK, FOURIER_WIDTH, N_BRANCHES * D_MODEL)
IN_WIDTH = (2 * GLA_KEY_WIDTH + 2 * GLA_VAL_WIDTH + 2 * GATE_RANK
            + FOURIER_WIDTH + N_BRANCHES * D_MODEL)


def rmsnorm(x, g):
    xf = x.astype(jnp.float32)
    y = xf * lax.rsqrt(jnp.mean(jnp.square(xf), axis=-1, keepdims=True) + EPS)
    return (y * g.astype(jnp.float32)).astype(x.dtype)

def modulate(h, shift, scale):
    return h * (1.0 + scale) + shift

def pos_embed_2d(n_tokens, dtype):
    rows = n_tokens // GRID_W
    row = jnp.repeat(jnp.arange(rows, dtype=jnp.float32), GRID_W)
    col = jnp.tile(jnp.arange(GRID_W, dtype=jnp.float32), rows)
    quarter = D_MODEL // 4
    omega = 1.0 / (POS_TEMP ** (jnp.arange(quarter, dtype=jnp.float32) / quarter))
    er = row[:, None] * omega[None, :]
    ec = col[:, None] * omega[None, :]
    return jnp.concatenate([jnp.sin(er), jnp.cos(er), jnp.sin(ec), jnp.cos(ec)], axis=-1).astype(dtype)

def split_proj(proj):
    parts = []
    start = 0
    for w in IN_SPLIT_WIDTHS:
        parts.append(proj[..., start:start + w])
        start += w
    return parts

def gla_inputs(parts, w_lr_f, b_lr_f, w_lr_b, b_lr_b):
    q, k, v, _, lr_f, lr_b, _, _ = parts
    b, n, _ = q.shape
    heads = lambda a, d: a.astype(jnp.float32).reshape(b, n, GLA_HEADS, d)
    q = heads(q, GLA_DK) * (GLA_DK ** -0.5)
    k = heads(k, GLA_DK)
    v = heads(v, GLA_DV)
    la_f = jax.nn.log_sigmoid((lr_f @ w_lr_f + b_lr_f).astype(jnp.float32)) / GATE_TAU
    la_b = jax.nn.log_sigmoid((lr_b @ w_lr_b + b_lr_b).astype(jnp.float32)) / GATE_TAU
    return q, k, v, heads(la_f, GLA_DK), heads(la_b, GLA_DK)

def gla_chunked(q, k, v, log_a, s0):
    b, t, h, dk = q.shape
    dv = v.shape[-1]
    n = t // CHUNK
    chunks = lambda a: a.reshape(b, n, CHUNK, h, a.shape[-1])
    q, k, v, log_a = chunks(q), chunks(k), chunks(v), chunks(log_a)
    cum = jnp.cumsum(log_a, axis=2)
    cum_last = cum[:, :, -1:]
    q_dec = q * jnp.exp(cum)
    k_inv = k * jnp.exp(-cum)
    k_end = k * jnp.exp(cum_last - cum)
    causal_in_scan = jnp.tril(jnp.ones((CHUNK, CHUNK), dtype=bool))
    scores = jnp.einsum('bnthd,bnshd->bnhts', q_dec, k_inv)
    scores = jnp.where(causal_in_scan, scores, 0.0)
    o_intra = jnp.einsum('bnhts,bnshv->bnthv', scores, v)

    def step(s, xs):
        qd, ke, vc, dec = xs
        o = jnp.einsum('bthd,bhdv->bthv', qd, s)
        s = dec[..., None] * s + jnp.einsum('bshd,bshv->bhdv', ke, vc)
        return s, o

    xs = (q_dec.swapaxes(0, 1), k_end.swapaxes(0, 1), v.swapaxes(0, 1),
          jnp.exp(cum_last[:, :, 0]).swapaxes(0, 1))
    s_final, o_inter = lax.scan(step, s0, xs)
    o = o_intra + o_inter.swapaxes(0, 1)
    return o.reshape(b, t, h, dv), s_final

def bidir_gla(q, k, v, la_f, la_b, s_f0, s_b0):
    o_f, s_f = gla_chunked(q, k, v, la_f, s_f0)
    flip = lambda a: jnp.flip(a, axis=1)
    o_b, s_b = gla_chunked(flip(q), flip(k), flip(v), flip(la_b), s_b0)
    return o_f + flip(o_b), s_f, s_b

def fourier_mix(u):
    b, n, _ = u.shape
    ug = u.astype(jnp.float32).reshape(b, n, FOURIER_GROUPS, FOURIER_GROUP_DIM)
    y = jnp.real(jnp.fft.fft2(ug, axes=(1, 3), norm='ortho'))
    return y.reshape(b, n, FOURIER_WIDTH).astype(u.dtype)

def merge_branches(parts, o_gla, gla_norm_g, w_fourier_out, w_gla_out, w_out):
    _, _, _, g_out, _, _, u_f, gates = parts
    b, n, _ = u_f.shape
    o = rmsnorm(o_gla, gla_norm_g).reshape(b, n, GLA_VAL_WIDTH).astype(u_f.dtype)
    y_gla = (o * jax.nn.silu(g_out)) @ w_gla_out
    y_fft = fourier_mix(u_f) @ w_fourier_out
    gate_fft, gate_gla = jnp.split(jax.nn.sigmoid(gates), N_BRANCHES, axis=-1)
    return (gate_fft * y_fft + gate_gla * y_gla) @ w_out

def sq_relu_mlp(h, w_in, w_out):
    return jnp.square(jax.nn.relu(h @ w_in)) @ w_out

def first_inputs(seed: int = 0) -> dict:
    key = jax.random.key(seed)
    ks = jax.random.split(key, 24)
    nrm = lambda k, shape, s: jax.random.normal(k, shape, jnp.float32) * s
    L = DEPTH
    return {
        "x": nrm(ks[0], (BATCH, SEQ, D_MODEL), 1.0),
        "c": nrm(ks[1], (BATCH, D_MODEL), 1.0),
        "ctx": nrm(ks[2], (BATCH, CTX_LEN, D_MODEL), 1.0),
        "c_ctx": nrm(ks[3], (D_MODEL,), 1.0),
        "w_mod": nrm(ks[4], (L, D_MODEL, N_MOD * D_MODEL), 0.5 * D_MODEL ** -0.5),
        "b_mod": nrm(ks[5], (L, N_MOD * D_MODEL), 0.02),
        "norm1_g": 1.0 + nrm(ks[6], (L, D_MODEL), 0.05),
        "norm2_g": 1.0 + nrm(ks[7], (L, D_MODEL), 0.05),
        "w_in": nrm(ks[8], (L, D_MODEL, IN_WIDTH), D_MODEL ** -0.5),
        "w_lr_f": nrm(ks[9], (L, GATE_RANK, GLA_KEY_WIDTH), GATE_RANK ** -0.5),
        "b_lr_f": nrm(ks[10], (L, GLA_KEY_WIDTH), 0.1),
        "w_lr_b": nrm(ks[11], (L, GATE_RANK, GLA_KEY_WIDTH), GATE_RANK ** -0.5),
        "b_lr_b": nrm(ks[12], (L, GLA_KEY_WIDTH), 0.1),
        "gla_norm_g": 1.0 + nrm(ks[13], (L, GLA_DV), 0.05),
        "w_fourier_out": nrm(ks[14], (L, FOURIER_WIDTH, D_MODEL), FOURIER_WIDTH ** -0.5),
        "w_gla_out": nrm(ks[15], (L, GLA_VAL_WIDTH, D_MODEL), GLA_VAL_WIDTH ** -0.5),
        "w_out": nrm(ks[16], (L, D_MODEL, D_MODEL), D_MODEL ** -0.5),
        "w_mlp_in": nrm(ks[17], (L, D_MODEL, D_FF), D_MODEL ** -0.5),
        "w_mlp_out": nrm(ks[18], (L, D_FF, D_MODEL), D_FF ** -0.5),
        "final_norm_g": 1.0 + nrm(ks[19], (D_MODEL,), 0.05),
    }

def first_block(x, c, ctx, c_ctx, w_mod, b_mod, norm1_g, norm2_g, w_in, w_lr_f, b_lr_f,
              w_lr_b, b_lr_b, gla_norm_g, w_fourier_out, w_gla_out, w_out, w_mlp_in,
              w_mlp_out, final_norm_g):
    b = x.shape[0]
    x = x + pos_embed_2d(x.shape[1], x.dtype)[None]
    x_ctx = ctx
    for i in range(DEPTH):
        last = i == DEPTH - 1
        mod_lat = jax.nn.silu(c) @ w_mod[i] + b_mod[i]
        mod_ctx = (jax.nn.silu(c_ctx) @ w_mod[i] + b_mod[i])[None]
        sh1, sc1, gt1, sh2, sc2, gt2 = [m[:, None] for m in jnp.split(mod_lat, N_MOD, axis=-1)]
        csh1, csc1, cgt1, csh2, csc2, cgt2 = [m[:, None] for m in jnp.split(mod_ctx, N_MOD, axis=-1)]

        h_ctx = modulate(rmsnorm(x_ctx, norm1_g[i]), csh1, csc1)
        parts_ctx = split_proj(h_ctx @ w_in[i])
        q_c, k_c, v_c, laf_c, lab_c = gla_inputs(parts_ctx, w_lr_f[i], b_lr_f[i], w_lr_b[i], b_lr_b[i])
        s_zero = jnp.zeros((b, GLA_HEADS, GLA_DK, GLA_DV), jnp.float32)
        o_ctx, s_f_ctx, s_b_ctx = bidir_gla(q_c, k_c, v_c, laf_c, lab_c, s_zero, s_zero)

        h = modulate(rmsnorm(x, norm1_g[i]), sh1, sc1)
        parts = split_proj(h @ w_in[i])
        q, k, v, la_f, la_b = gla_inputs(parts, w_lr_f[i], b_lr_f[i], w_lr_b[i], b_lr_b[i])
        o_lat, _, _ = bidir_gla(q, k, v, la_f, la_b, s_f_ctx, s_b_ctx)
        y = merge_branches(parts, o_lat, gla_norm_g[i], w_fourier_out[i], w_gla_out[i], w_out[i])
        x = x + gt1 * y

        h2 = modulate(rmsnorm(x, norm2_g[i]), sh2, sc2)
        x = x + gt2 * sq_relu_mlp(h2, w_mlp_in[i], w_mlp_out[i])

        if not last:
            y_ctx = merge_branches(parts_ctx, o_ctx, gla_norm_g[i], w_fourier_out[i], w_gla_out[i], w_out[i])
            x_ctx = x_ctx + cgt1 * y_ctx
            h2_ctx = modulate(rmsnorm(x_ctx, norm2_g[i]), csh2, csc2)
            x_ctx = x_ctx + cgt2 * sq_relu_mlp(h2_ctx, w_mlp_in[i], w_mlp_out[i])

    return rmsnorm(x, final_norm_g)


HEAD_DIM = 128
D_MIX = D_MODEL
W_A = 6 * HEAD_DIM
W_B = 6 * HEAD_DIM
N_POOL_GROUPS = 4
POOL_WINDOWS = (2, 4, 8, 16)
G_C = HEAD_DIM
W_C = N_POOL_GROUPS * G_C
D_IN_TOT = 3 * W_A + 2 * W_B + W_C
K_SHORT = 3
K_CONFORMER = 31
K_FFN = 3
D_FF_2 = 5632
RMS_EPS = 1e-6
LN_EPS = 1e-5


def rms_norm(x, g):
    xf = x.astype(jnp.float32)
    y = xf * lax.rsqrt(jnp.mean(xf * xf, axis=-1, keepdims=True) + RMS_EPS)
    return (y * g.astype(jnp.float32)).astype(x.dtype)

def layer_norm(x, g, b):
    xf = x.astype(jnp.float32)
    mu = jnp.mean(xf, axis=-1, keepdims=True)
    var = jnp.mean(jnp.square(xf - mu), axis=-1, keepdims=True)
    y = (xf - mu) * lax.rsqrt(var + LN_EPS)
    return (y * g.astype(jnp.float32) + b.astype(jnp.float32)).astype(x.dtype)

def causal_depthwise_conv(x, w):
    k, c = w.shape
    return lax.conv_general_dilated(
        x, w[:, None, :].astype(x.dtype),
        window_strides=(1,), padding=[(k - 1, 0)],
        dimension_numbers=("NWC", "WIO", "NWC"),
        feature_group_count=c)

def trailing_mean_minus_self(x, window):
    s = x.shape[1]
    xf = x.astype(jnp.float32)
    c = jnp.cumsum(xf, axis=1)
    c_shift = jnp.pad(c, ((0, 0), (window, 0), (0, 0)))[:, :s]
    counts = jnp.minimum(jnp.arange(1, s + 1, dtype=jnp.float32), float(window))[None, :, None]
    return ((c - c_shift) / counts - xf).astype(x.dtype)

def short_gated_conv_mixer(u_a, conv_w):
    b_gate, c_gate, v = jnp.split(u_a, 3, axis=-1)
    return b_gate * causal_depthwise_conv(c_gate * v, conv_w)

def conformer_conv_mixer(u_b, conv_w, conv_b, ln_g, ln_b):
    val, gate = jnp.split(u_b, 2, axis=-1)
    glu = val * jax.nn.sigmoid(gate)
    y = causal_depthwise_conv(glu, conv_w) + conv_b
    y = layer_norm(y, ln_g, ln_b)
    return jax.nn.silu(y)

def multiscale_pool_mixer(u_c, pool_w, pool_scale):
    bsz, s, _ = u_c.shape
    groups = u_c.reshape(bsz, s, N_POOL_GROUPS, G_C)
    pooled = jnp.stack(
        [trailing_mean_minus_self(groups[:, :, gi], w) for gi, w in enumerate(POOL_WINDOWS)],
        axis=2)
    mixed = jnp.einsum("bsgc,gcd->bsgd", pooled, pool_w)
    return mixed.reshape(bsz, s, W_C) * pool_scale

def conv_gated_mlp(h, w_up, conv_w, conv_b, w_down):
    up = h @ w_up
    up = causal_depthwise_conv(up, conv_w) + conv_b
    gate, val = jnp.split(up, 2, axis=-1)
    return (jax.nn.silu(gate) * val) @ w_down

def second_inputs(seed: int = 0) -> dict:
    key = jax.random.key(seed)
    ks = jax.random.split(key, 20)
    f32 = jnp.float32
    nrm = lambda k, shape, scale: jax.random.normal(k, shape, f32) * scale
    gain = lambda k, shape: 1.0 + 0.05 * jax.random.normal(k, shape, f32)
    return {
        "x": jax.random.normal(ks[0], (BATCH, SEQ, D_MODEL), f32),
        "norm_mix_pre": gain(ks[1], (DEPTH, D_MODEL)),
        "norm_mix_post": gain(ks[2], (DEPTH, D_MODEL)),
        "norm_ffn_pre": gain(ks[3], (DEPTH, D_MODEL)),
        "norm_ffn_post": gain(ks[4], (DEPTH, D_MODEL)),
        "w_in": nrm(ks[5], (DEPTH, D_MODEL, D_IN_TOT), D_MODEL ** -0.5),
        "conv_a_w": nrm(ks[6], (DEPTH, K_SHORT, W_A), K_SHORT ** -0.5),
        "conv_b_w": nrm(ks[7], (DEPTH, K_CONFORMER, W_B), K_CONFORMER ** -0.5),
        "conv_b_bias": nrm(ks[8], (DEPTH, W_B), 0.01),
        "ln_b_gain": gain(ks[9], (DEPTH, W_B)),
        "ln_b_bias": nrm(ks[10], (DEPTH, W_B), 0.01),
        "pool_w": nrm(ks[11], (DEPTH, N_POOL_GROUPS, G_C, G_C), G_C ** -0.5),
        "pool_scale": 1.0 + 0.1 * jax.random.normal(ks[12], (DEPTH, W_C), f32),
        "w_out": nrm(ks[13], (DEPTH, D_MIX, D_MODEL), D_MIX ** -0.5),
        "w_up": nrm(ks[14], (DEPTH, D_MODEL, 2 * D_FF_2), D_MODEL ** -0.5),
        "conv_ffn_w": nrm(ks[15], (DEPTH, K_FFN, 2 * D_FF_2), K_FFN ** -0.5),
        "conv_ffn_bias": nrm(ks[16], (DEPTH, 2 * D_FF_2), 0.01),
        "w_down": nrm(ks[17], (DEPTH, D_FF_2, D_MODEL), D_FF_2 ** -0.5),
    }

def second_block(x, norm_mix_pre, norm_mix_post, norm_ffn_pre, norm_ffn_post,
              w_in, conv_a_w, conv_b_w, conv_b_bias, ln_b_gain, ln_b_bias,
              pool_w, pool_scale, w_out, w_up, conv_ffn_w, conv_ffn_bias, w_down):
    for l in range(DEPTH):
        h = rms_norm(x, norm_mix_pre[l])
        u = h @ w_in[l]
        u_a = u[..., :3 * W_A]
        u_b = u[..., 3 * W_A:3 * W_A + 2 * W_B]
        u_c = u[..., 3 * W_A + 2 * W_B:]
        y_a = short_gated_conv_mixer(u_a, conv_a_w[l])
        y_b = conformer_conv_mixer(u_b, conv_b_w[l], conv_b_bias[l], ln_b_gain[l], ln_b_bias[l])
        y_c = multiscale_pool_mixer(u_c, pool_w[l], pool_scale[l])
        y = jnp.concatenate([y_a, y_b, y_c], axis=-1) @ w_out[l]
        x = x + rms_norm(y, norm_mix_post[l])
        h = rms_norm(x, norm_ffn_pre[l])
        f = conv_gated_mlp(h, w_up[l], conv_ffn_w[l], conv_ffn_bias[l], w_down[l])
        x = x + rms_norm(f, norm_ffn_post[l])
    return x


def setup_inputs(seed=0):
    out = dict(first_inputs(seed))
    for name, value in second_inputs(seed + 1).items():
        if name != "x":
            out[name + "_2"] = value
    return out


def reference(
    x, c, ctx, c_ctx, w_mod, b_mod, norm1_g, norm2_g, w_in, w_lr_f, b_lr_f, w_lr_b, b_lr_b,
    gla_norm_g, w_fourier_out, w_gla_out, w_out, w_mlp_in, w_mlp_out, final_norm_g,
    norm_mix_pre_2, norm_mix_post_2, norm_ffn_pre_2, norm_ffn_post_2, w_in_2, conv_a_w_2,
    conv_b_w_2, conv_b_bias_2, ln_b_gain_2, ln_b_bias_2, pool_w_2, pool_scale_2, w_out_2,
    w_up_2, conv_ffn_w_2, conv_ffn_bias_2, w_down_2,
):
    x = first_block(
        x, c, ctx, c_ctx, w_mod, b_mod, norm1_g, norm2_g, w_in, w_lr_f, b_lr_f, w_lr_b, b_lr_b,
        gla_norm_g, w_fourier_out, w_gla_out, w_out, w_mlp_in, w_mlp_out, final_norm_g,
    )
    return second_block(
        x, norm_mix_pre_2, norm_mix_post_2, norm_ffn_pre_2, norm_ffn_post_2, w_in_2, conv_a_w_2,
        conv_b_w_2, conv_b_bias_2, ln_b_gain_2, ln_b_bias_2, pool_w_2, pool_scale_2, w_out_2,
        w_up_2, conv_ffn_w_2, conv_ffn_bias_2, w_down_2,
    )


_drawn_inputs = setup_inputs


def setup_inputs(seed=0):
    import zlib

    import numpy as np

    out = dict(_drawn_inputs(seed))
    spreads = {}
    factors = {'ctx': 3.048,
     'c_ctx': 4.659,
     'norm1_g': 2.803,
     'b_lr_f': 7.175,
     'b_lr_b': 8.0,
     'gla_norm_g': 7.379,
     'conv_b_bias_2': 5.937,
     'ln_b_bias_2': 8.0,
     'conv_ffn_bias_2': 6.973,
     'norm2_g': 4.602}
    for name, (base, spread) in spreads.items():
        noise = np.random.default_rng([zlib.crc32(name.encode()), seed]).standard_normal(out[name].shape)
        drawn = base * np.exp(spread * noise) if base else spread * noise
        out[name] = __import__('jax').numpy.asarray(drawn.astype(out[name].dtype))
    for name, factor in factors.items():
        out[name] = (out[name] * factor).astype(out[name].dtype)
    return out
```

```python
import concourse.bass as bass
from concourse import mybir
from contextlib import ExitStack

P = 128
D = 2048
NT = 256
KT = D // P
GC = 512
NSLOT = 4
MODS = 6
HEADS, DK, DV = 4, 128, 256
KEYW, VALW, RANK = HEADS * DK, HEADS * DV, 16
CHUNK = 64
FGROUPS, FDIM = 4, 256
C_Q, C_K, C_V = 0, KEYW, 2 * KEYW
C_GOUT = 2 * KEYW + VALW
C_LR = C_GOUT + VALW
C_U = C_LR + 2 * RANK
C_GFFT = C_U + FGROUPS * FDIM
C_GGLA = C_GFFT + D
EPS = 1e-6
LN_EPS = 1e-5
MLP_CHUNKS = 4 * D // 2048
WA, WB, WC = 768, 768, 512
TA, TB, TC = WA // P, WB // P, WC // P
C2_B, C2_C = 3 * WA, 3 * WA + 2 * WB
UT = (C2_C + WC) // P
KCONV = 31
FF2 = 5632
FT = FF2 // P
PROWS = [("c", KT), ("c_ctx", KT), ("b_mod", MODS * KT), ("norm1_g", KT), ("norm2_g", KT),
         ("final_norm_g", KT), ("norm_mix_pre_2", KT), ("norm_mix_post_2", KT), ("norm_ffn_pre_2", KT),
         ("norm_ffn_post_2", KT), ("gla_norm_g", DV // P), ("conv_a_w_2", 3 * TA),
         ("conv_b_w_2", KCONV * TB), ("conv_b_bias_2", TB), ("ln_b_gain_2", TB), ("ln_b_bias_2", TB),
         ("pool_scale_2", TC), ("conv_ffn_w_2", 3 * 2 * FT), ("conv_ffn_bias_2", 2 * FT)]
COL, _n = {}, 0
for _name, _rows in PROWS:
    COL[_name] = _n
    _n += _rows
NPARAM = _n
NPB = -(-NPARAM // P)
NPDMA = sum((COL[n] + r - 1) // P - COL[n] // P + 1 for n, r in PROWS)
NCON = P + 4 * 16
NORMS_BEFORE = [2, 2, 3, 5, 7]


class Turns:

    def __init__(self, u=(0, 0, 0, 0), f=(0, 0)):
        self.u, self.f = list(u), list(f)

    def inside(self, i, uses, frees):
        return Turns([a + i * uses for a in self.u], [a + i * b for a, b in zip(self.f, frees)])

    def passed(self, n, uses, frees):
        self.u = [a + n * uses for a in self.u]
        self.f = [a + n * b for a, b in zip(self.f, frees)]


def build(nc, ins, out):
    f32, f32r, u32 = mybir.dt.float32, mybir.dt.float32r, mybir.dt.uint32
    ALU, ACT = mybir.AluOpType, mybir.ActivationFunctionType
    ds = bass.ds

    ctx = ExitStack()
    with ctx:
        def sb(name, shape, dt=f32):
            return ctx.enter_context(nc.sbuf_tensor(name, shape, dt))

        def sem(name):
            return ctx.enter_context(nc.semaphore(name))

        def overlay(hold, nbytes, *tensors):
            made = []
            for group in tensors:
                with ExitStack() as own:
                    made += [own.enter_context(nc.sbuf_tensor(n, s, d)) for n, s, d in group]
            sb(hold, [P, nbytes // 4])
            return made

        raw = sb("raw", [P, NSLOT, 4, GC])
        whi = sb("whi", [P, 4, 2, GC], f32r)
        wlo = sb("wlo", [P, 4, 2, GC], f32r)
        hh = sb("hh", [P, KT, NT], f32r)
        hl = sb("hl", [P, KT, NT], f32r)
        tmp = sb("tmp", [P, 2, 4 * NT])
        wmr = sb("wmr", [P, 2, 2, GC])
        wacc = sb("wacc", [P, GC])
        par = sb("par", [P, NPARAM])
        con = sb("con", [P, NCON])
        ones = sb("ones", [P, P])
        rstd = sb("rstd", [P, 2, NT])
        root = sb("root", [P, NT])
        eps = sb("eps", [P, 2])
        csil = sb("csil", [P, 2, KT])
        cv = sb("cv", [P, KT, 4], f32r)
        mpre = sb("mpre", [P, 2, 2, KT])
        mods = sb("mods", [P, 4 * KT])
        a2 = sb("a2", [P, KT])
        fixed = sb("fixed", [P, 4, 16])
        oss = sb("oss", [P, 2, 2 * HEADS])
        (stage_x, posT, ch, cl, lab, keb, tq, state, dft, mh, ml) = overlay(
            "region_a", 32768,
            [("stage_x", [P, 2, D], f32), ("posT", [P, KT, NT], f32)],
            [("ch", [P, KT, NT], f32r), ("cl", [P, KT, NT], f32r)],
            [("lab", [P, 2, KEYW], f32), ("keb", [P, 2, KEYW], f32), ("tq", [P, 2, KEYW], f32),
             ("state", [P, 2, HEADS, DV], f32), ("dft", [P, 2, 2 * NT], f32)],
            [("mh", [P, KT, NT], f32r), ("ml", [P, KT, NT], f32r)])
        (xT, kiT, qdT, sT, wlr, lrn, lrT, dec, con2, yfh, yfl, xT2) = overlay(
            "region_x", 16384,
            [("xT", [P, KT, NT], f32)],
            [("kiT", [P, HEADS * P], f32), ("qdT", [P, HEADS * P], f32), ("sT", [P, 2, HEADS * P], f32),
             ("wlr", [RANK + 1, 2, KEYW], f32), ("lrn", [P, 4, 2, 32], f32), ("lrT", [RANK + 1, P], f32),
             ("dec", [P, HEADS, 2], f32), ("con2", [P, 4 * P + 2], f32)],
            [("yfh", [P, 8, NT], f32r), ("yfl", [P, 8, NT], f32r)],
            [("xT2", [P, KT, NT], f32)])
        (stage_c, ctxT, mraw, msum, csig, qn, kn, vn, un, ckn, cvn, oh, ol, sg, osb, pbuf, uT, cacc, yT, up1, up2, outn) = overlay(
            "region_b", 36864,
            [("stage_c", [P, 2, D], f32), ("ctxT", [P, KT, NT], f32), ("mraw", [P, 2 * KT, 4], f32),
             ("msum", [P, 2 * KT, 2], f32), ("csig", [P, 2, KT], f32)],
            [("qn", [P, 2, KEYW], f32), ("kn", [P, 2, KEYW], f32), ("vn", [P, 2, VALW], f32),
             ("un", [P, 2, 1024], f32), ("ckn", [P, 2, KEYW], f32), ("cvn", [P, 2, VALW], f32)],
            [("oh", [P, 8, NT], f32r), ("ol", [P, 8, NT], f32r), ("sg", [P, 8, NT], f32),
             ("osb", [P, 2, VALW], f32), ("pbuf", [P, 2, 2 * NT], f32)],
            [("uT", [P, UT, NT], f32), ("cacc", [P, 2, NT], f32)],
            [("yT", [P, KT, NT], f32), ("up1", [P, 4, NT], f32), ("up2", [P, 4, NT], f32)],
            [("outn", [P, 2, D], f32)])
        spill = nc.dram_tensor("spill", [P, KT * NT], f32, kind="Internal").ap()

        acc = [ctx.enter_context(nc.psum_tensor(f"acc{i}", [P, 4 * NT], f32)) for i in range(2)]
        mp = [ctx.enter_context(nc.psum_tensor(f"mp{i}", [P, 4 * NT], f32)) for i in range(2)]
        ident = con[:, 0:P]
        fix_w = con[:, P:NCON].rearrange("p (g t) -> p g t", g=4)
        cum_w = [con2[:, d * P:(1 + d) * P] for d in range(2)]
        end_w = [con2[:, (2 + d) * P:(3 + d) * P] for d in range(2)]
        half_w = con2[:, 4 * P:4 * P + 2]
        tiles = lambda ap: ap.rearrange("p (t n) -> p t n", n=NT)
        pcol = lambda name, i=0, n=1: par[:, COL[name] + i:COL[name] + i + n]

        raw_full = [sem(f"raw_full{s}") for s in range(NSLOT)]
        hi_done = [sem(f"hi_done{s}") for s in range(NSLOT)]
        lo_done = [sem(f"lo_done{s}") for s in range(NSLOT)]
        used = [sem(f"used{s}") for s in range(NSLOT)]
        acc_free = [sem(f"acc_free{i}") for i in range(2)]
        names = """par_in con_in x_in ctx_in par_ps par_sb csig_ok csil_ok chi_ok cv_ok xt_ps xt_sb ct_sb
            sq_ok ms_ok rt_ok rs_ok tm_ok t2_ok hi_ok lo_ok mod_a mod_b eps_ok spill_ok gla_in mac_ok
            red_ps mods_ok nat_v a_self v_self
            lrT_ps lrT_sb z_ps ln_ok la_ok cum_ps kexp_ok qexp_ok ke_ok qk_ok qkT_ps qkT_sb sc_ps sc_sb u_ps
            st_ok o_ok oss_ok ort_ok ons_ok oT_ps ot_ok ohi_ok olo_ok p_ps p_sb y_ps yhi_ok ylo_ok
            sg_a mt_ok mhi_ok mlo_ok x_back sg_v relu_ok rsq_ok hhi_ok hid_ok
            bsig_ok tap_ok a_ok mxh_ok mxl_ok pooled_ok pool_ps pool_sb pw_in ln_d ln_sq ln_ps ln_rt
            ln_z ln_sg vt_ok ct_ok cd_ok gs_ok gm_ok fhi_ok fid_ok gate_ok mrg_ok tap2_ok gu_ok out_ps out_sb stored""".split()
        S = {n: sem(n) for n in names}
        wm_in = [sem(f"wm_in{i}") for i in range(2)]

        block = ctx.enter_context(nc.Block())

        def load(sp, st, w, row0, col0, width=GC, slots=4, srcs=None):
            for s in range(slots):
                src, r = srcs[s] if srcs else (w, row0 + 512 * s)
                if not (isinstance(st.u[s], int) and st.u[s] == 0):
                    sp.wait_ge(lo_done[s], 2 * st.u[s])
                rows = src[ds(r, 512), ds(col0, width)].rearrange("(k p) n -> p k n", p=P)
                sp.dma_start(raw[:, s, :, 0:width], rows).then_inc(raw_full[s], 16)
                st.u[s] = st.u[s] + 1

        def pieces(slots):
            return [(s, j, (2 * s + j) % 4) for s in slots for j in range(2)]

        def conv_hi(act, st, slots, width=GC, after3=False):
            for s, j, r in pieces(slots):
                o = (s + 2) % 4
                if j == 0:
                    act.wait_ge(raw_full[s], 16 * st.u[s] + 16)
                if not (isinstance(st.u[o], int) and st.u[o] == 0):
                    act.wait_ge(used[o], 2 * st.u[o] - 1 + j)
                if after3 and s == 1:
                    act.wait_ge(used[s], 2 * st.u[s] - 1 + j)
                nc.scalar.activation(whi[:, r, :, 0:width], raw[:, s, 2 * j:2 * j + 2, 0:width],
                                     ACT.Copy).then_inc(hi_done[s], 1)
                if j == 1:
                    st.u[s] = st.u[s] + 1

        def conv_lo(dve, st, slots, width=GC, mac=None):
            for n, (s, j, r) in enumerate(pieces(slots)):
                dve.wait_ge(hi_done[s], 2 * st.u[s] + j + 1)
                nc.vector.tensor_tensor(wlo[:, r, :, 0:width], raw[:, s, 2 * j:2 * j + 2, 0:width],
                                        whi[:, r, :, 0:width].bitcast(f32),
                                        ALU.subtract).then_inc(lo_done[s], 1)
                if j == 1:
                    st.u[s] = st.u[s] + 1
                if mac:
                    mac(n)

        def split_ahead(conv, st, slots=4, nslots=4, width=GC, nwidth=GC, last=False, **kw):
            if slots > 2:
                conv(st, range(2, slots), width, **kw)
            if not last:
                conv(st, range(min(2, nslots)), nwidth, **kw)

        def group_done(eng, st, slots=4):
            eng.wait_ge(used[slots - 1], 2 * st.u[slots - 1])

        def mm_feature(pe, st, i, hi, lo, frees, slots=4, first=0, ntile=4, into=None, ready=None,
                       which=None, free=None):
            which = range(slots) if which is None else which
            if free:
                pe.wait_ge(*free)
            else:
                pe.wait_ge(acc_free[i], st.f[i])
            for n, s in enumerate(which):
                if ready:
                    ready(n)
                for j in range(2):
                    r = (2 * s + j) % 4
                    pe.wait_ge(lo_done[s], 2 * st.u[s] + j + 1)
                    for k in range(2):
                        kt = first + 4 * n + 2 * j + k
                        for t in range(ntile):
                            dst = acc[i][:, t * NT:(t + 1) * NT]
                            cols = slice(t * P, (t + 1) * P)
                            begin = kt == first and t % 2 == 0
                            nc.tensor.matmul(dst, whi[:, r, k, cols], hi[:, kt, :], start=begin, stop=False,
                                             skip_group_check=True)
                            nc.tensor.matmul(dst, whi[:, r, k, cols], lo[:, kt, :], start=False, stop=False,
                                             skip_group_check=True)
                            last = nc.tensor.matmul(dst, wlo[:, r, k, cols], hi[:, kt, :], start=False,
                                                    stop=kt == first + 4 * len(which) - 1,
                                                    skip_group_check=True)
                    last.then_inc(used[s], 1)
                st.u[s] = st.u[s] + 1
            st.f[i] = st.f[i] + frees

        def mm_token(pe, st, i, width, with_ctx, ready=None):
            if st.f[i]:
                pe.wait_ge(acc_free[i], st.f[i])
            outs = [(acc[i], 0, hh, hl, 0, width), (acc[i], GC, hh, hl, P, width)]
            if with_ctx:
                outs += [(mp[i], 0, ch, cl, 0, with_ctx), (mp[i], GC, ch, cl, P, with_ctx)]
            for s in range(4):
                if ready:
                    ready(s)
                for j in range(2):
                    r = (2 * s + j) % 4
                    pe.wait_ge(lo_done[s], 2 * st.u[s] + j + 1)
                    for k in range(2):
                        kt = 4 * s + 2 * j + k
                        for bank, off, hi, lo, t0, w in outs:
                            dst = bank[:, off:off + w]
                            nc.tensor.matmul(dst, hi[:, kt, t0:t0 + P], whi[:, r, k, 0:w], start=kt == 0,
                                             stop=False)
                            nc.tensor.matmul(dst, hi[:, kt, t0:t0 + P], wlo[:, r, k, 0:w], start=False,
                                             stop=False)
                            last = nc.tensor.matmul(dst, lo[:, kt, t0:t0 + P], whi[:, r, k, 0:w],
                                                    start=False, stop=kt == KT - 1)
                    last.then_inc(used[s], 1)
                st.u[s] += 1
            st.f[i] += 2 if with_ctx else 1

        TOKEN = [(C_K, GC, GC), (C_V, GC, GC), (C_V + GC, GC, GC), (C_LR, GC, 2 * RANK), (C_Q, GC, 0),
                 (C_LR + GC, GC, 0), (C_LR + 2 * GC, C_GFFT - C_LR - 2 * GC, 0)]
        NEXT_W = [w for _, w, _ in TOKEN[1:]] + [GC]
        F_TOKEN = [4 + sum(2 if cw else 1 for n, (_, _, cw) in enumerate(TOKEN) if n % 2 == i) for i in range(2)]
        F_OUT = [f + 2 for f in F_TOKEN]
        F_MLP = [f + 2 * MLP_CHUNKS for f in F_OUT]
        F_UB = [f + 2 for f in F_MLP]
        F_U = [F_UB[0] + 3, F_UB[1] + 2]
        F_OUT2 = [f + 2 for f in F_U]
        F_FFN = [f + 6 for f in F_OUT2]

        def all_read(eng, counts):
            for i in range(2):
                eng.wait_ge(acc_free[i], counts[i])

        SCANS = [(src, d, t) for src in range(2) for d in range(2) for t in ((0, 1), (1, 0))[d]]

        def norm_squares(act, k, src):
            for q in range(4):
                n = 4 * k + q
                if n >= 2:
                    act.wait_ge(S["ms_ok"], n - 1)
                nc.scalar.activation(tiles(tmp[:, q % 2, :]), src[:, 4 * q:4 * q + 4, :], ACT.Square)\
                    .then_inc(S["sq_ok"], 1)

        def norm_sums(pe, k, bank):
            for q in range(4):
                pe.wait_ge(S["sq_ok"], 4 * k + q + 1)
                for t in range(4):
                    last = nc.tensor.matmul(bank[:, 0:NT], ones[:, :], tmp[:, q % 2, t * NT:(t + 1) * NT],
                                            start=q + t == 0, stop=q + t == 6)
                last.then_inc(S["ms_ok"], 1)

        def norm_root(act, k, bank, n=D, e=0):
            act.wait_ge(S["ms_ok"], 4 * k + 4)
            if k:
                act.wait_ge(S["rs_ok"], k)
            nc.scalar.activation(root[:, :], bank[:, 0:NT], ACT.Sqrt, bias=eps[:, e:e + 1],
                                 scale=1.0 / n).then_inc(S["rt_ok"], 1)

        def norm_rstd(dve, k):
            dve.wait_ge(S["rt_ok"], k + 1)
            nc.vector.reciprocal(rstd[:, k % 2, :], root[:, :]).then_inc(S["rs_ok"], 1)

        def rbc(k, n=4):
            return rstd[:, k % 2:k % 2 + 1, :].to_broadcast([P, n, NT])

        def apply_dve(dve, a, k, src, lo, hi):
            def times(q):
                n = 4 * a + q
                if q == 0:
                    dve.wait_ge(S["rs_ok"], k + 1)
                    dve.wait_ge(S["ms_ok"], 4 * NORMS_BEFORE[a])
                if n >= 2:
                    dve.wait_ge(S["lo_ok"], n - 1)
                nc.vector.tensor_tensor(tiles(tmp[:, q % 2, :]), src[:, 4 * q:4 * q + 4, :], rbc(k),
                                        ALU.mult).then_inc(S["tm_ok"], 1)

            def rest(q):
                dve.wait_ge(S["hi_ok"], 4 * a + q + 1)
                nc.vector.tensor_tensor(lo[:, 4 * q:4 * q + 4, :], tiles(tmp[:, q % 2, :]),
                                        hi[:, 4 * q:4 * q + 4, :].bitcast(f32),
                                        ALU.subtract).then_inc(S["lo_ok"], 1)
            times(0)
            for q in range(4):
                if q < 3:
                    times(q + 1)
                rest(q)

        def apply_act(act, a, hi, scale, shift):
            for q in range(4):
                n = 4 * a + q
                act.wait_ge(S["tm_ok"], n + 1)
                for t in range(4):
                    kt = 4 * q + t
                    part = tmp[:, q % 2, t * NT:(t + 1) * NT]
                    last = nc.scalar.activation(part, part, ACT.Identity,
                                                bias=shift(kt) if shift else 0.0, scale=scale(kt))
                last.then_inc(S["t2_ok"], 1)
                act.wait_ge(S["t2_ok"], n + 1)
                nc.scalar.activation(hi[:, 4 * q:4 * q + 4, :], tiles(tmp[:, q % 2, :]), ACT.Copy)\
                    .then_inc(S["hi_ok"], 1)

        def h_ready(pe, a, n=1):
            def wait(s):
                pe.wait_ge(S["lo_ok"], 4 * (a + n - 1) + s + 1)
            return wait

        @block.sync
        def _(sp):
            rows = tmp[:, 0, 0:NPB * P].rearrange("p (b n) -> p b n", b=NPB)
            for name, n in PROWS:
                done = 0
                while done < n:
                    r = COL[name] + done
                    m = min(n - done, P - r % P)
                    sp.dma_start(rows[r % P:r % P + m, r // P, :], ins[name][done:done + m, :])\
                        .then_inc(S["par_in"], 16)
                    done += m
            st = Turns()
            load(sp, st, ins["w_mod"], 0, 0)
            with sp.Fori(0, 7) as g:
                load(sp, st.inside(g, 1, (0, 0)), ins["w_mod"], 0, GC * g + GC)
            st.passed(7, 1, (0, 0))
            for c0, width, _ in TOKEN:
                load(sp, st, ins["w_in"], 0, c0, width)
            for g in range(2):
                load(sp, st, ins["w_in"], 0, C_GOUT + GC * g)
            with sp.Fori(1, 5) as j:
                it = st.inside(j - 1, 3, (0, 0))
                load(sp, it, ins["w_in"], 0, C_GFFT - GC + GC * j)
                load(sp, it, ins["w_in"], 0, C_GGLA - GC + GC * j)
                load(sp, it, None, 0, GC * j - GC, srcs=[(ins["w_fourier_out"], 0), (ins["w_fourier_out"], 512),
                                                    (ins["w_gla_out"], 0), (ins["w_gla_out"], 512)])
            st.passed(4, 3, (0, 0))
            with sp.Fori(0, 4) as g:
                load(sp, st.inside(g, 1, (0, 0)), ins["w_out"], 0, GC * g)
            st.passed(4, 1, (0, 0))
            with sp.Fori(0, MLP_CHUNKS) as c:
                it = st.inside(c, 8, (0, 0))
                for g in range(4):
                    load(sp, it, ins["w_mlp_in"], 0, 2048 * c + GC * g)
                for g in range(4):
                    load(sp, it, ins["w_mlp_out"], 2048 * c, GC * g)
            st.passed(MLP_CHUNKS, 8, (0, 0))
            with sp.Fori(0, 4) as g:
                load(sp, st.inside(g, 1, (0, 0)), ins["w_in_2"], 0, C2_B + GC * g)
            st.passed(4, 1, (0, 0))
            with sp.Fori(0, 4) as g:
                load(sp, st.inside(g, 1, (0, 0)), ins["w_in_2"], 0, GC * g)
            st.passed(4, 1, (0, 0))
            load(sp, st, ins["w_in_2"], 0, 4 * GC, C2_B - 4 * GC)
            with sp.Fori(0, 4) as g:
                load(sp, st.inside(g, 1, (0, 0)), ins["w_out_2"], 0, GC * g)
            st.passed(4, 1, (0, 0))

            def ffn(it, c, pairs, slots):
                for p in range(pairs):
                    load(sp, it, ins["w_up_2"], 0, 2048 * c + GC * p)
                    load(sp, it, ins["w_up_2"], 0, FF2 + 2048 * c + GC * p)
                for g in range(4):
                    load(sp, it, ins["w_down_2"], 2048 * c, GC * g, slots=slots)
            with sp.Fori(0, 2) as c:
                ffn(st.inside(c, 12, (0, 0)), c, 4, 4)
            st.passed(2, 12, (0, 0))
            ffn(st, 2, 3, 3)
            sp.wait_ge(S["out_sb"], 4)
            sp.dma_start(out.rearrange("(t p) d -> p t d", p=P), outn[:, :, :]).then_inc(S["stored"], 16)
            sp.wait_ge(S["stored"], 16)

        @block.gpsimd
        def _(pool):
            pool.wait_ge(S["xt_sb"], 4)
            pool.dma_start(spill, xT[:, :, :].rearrange("p t n -> p (t n)")).then_inc(S["spill_ok"], 16)
            pool.wait_ge(S["spill_ok"], 16)
            pool.wait_ge(S["lo_ok"], 4)
            for d, (w, b) in enumerate((("w_lr_f", "b_lr_f"), ("w_lr_b", "b_lr_b"))):
                pool.dma_start(wlr[0:RANK, d, :], ins[w]).then_inc(S["gla_in"], 16)
                pool.dma_start(wlr[RANK:RANK + 1, d, :], ins[b]).then_inc(S["gla_in"], 16)
            pool.dma_start(con2[:, :], ins["con2"]).then_inc(S["gla_in"], 16)
            pool.wait_ge(S["nat_v"], 4)
            pool.dma_start(dft[:, :, :], ins["dft"].rearrange("(t p) n -> p t n", p=P))\
                .then_inc(S["gla_in"], 16)

            def piece(w, p):
                n = 8 * w + p
                if not isinstance(w, int) or w or p >= 2:
                    pool.wait_ge(S["mac_ok"], 2 * n - 2)
                src = ins["w_mod"][2 * p * P:(2 * p + 2) * P, ds(2 * D + GC * w, GC)]
                pool.dma_start(wmr[:, p % 2, :, :], src.rearrange("(k p) n -> p k n", p=P))\
                    .then_inc(wm_in[p % 2], 16)
            for p in range(8):
                piece(0, p)
            with pool.Fori(1, 12) as w:
                for p in range(8):
                    piece(w, p)
            pool.wait_ge(S["mlo_ok"], 5)
            pool.dma_start(xT2[:, :, :].rearrange("p t n -> p (t n)"), spill).then_inc(S["x_back"], 16)
            with pool.Fori(12, 16) as w:
                for p in range(8):
                    piece(w, p)
            pool.wait_ge(S["mods_ok"], 17)
            pool.dma_start(wacc[:, :].rearrange("p (g d) -> p g d", g=TC),
                           ins["pool_w_2"].rearrange("(g p) d -> p g d", p=P)).then_inc(S["pw_in"], 16)

        @block.scalar
        def _(act):
            act.dma_start(con[:, :], ins["con"]).then_inc(S["con_in"], 16)
            act.dma_start(stage_x[:, :, :], ins["x"].rearrange("(t p) d -> p t d", p=P)).then_inc(S["x_in"], 16)
            act.dma_start(posT[:, :, :].rearrange("p t n -> p (t n)"), ins["posT"]).then_inc(S["x_in"], 16)
            act.dma_start(stage_c[:, :, :], ins["ctx"].rearrange("(t p) d -> p t d", p=P))\
                .then_inc(S["ctx_in"], 16)
            st = Turns()

            def own(n):
                act.wait_ge(S["a_self"], n)

            act.wait_ge(S["par_sb"], 1)
            nc.scalar.activation(csig[:, :, :], pcol("c", 0, 2 * KT).rearrange("p (v k) -> p v k", v=2),
                                 ACT.Sigmoid).then_inc(S["csig_ok"], 1)
            act.wait_ge(S["csil_ok"], 1)
            nc.scalar.activation(cv[:, :, 0:2], csil[:, :, :].rearrange("p v k -> p k v"), ACT.Copy)\
                .then_inc(S["chi_ok"], 1)
            conv_hi(act, st, (0, 1))
            for g in range(2):
                split_ahead(lambda *a, **k: conv_hi(act, *a, **k), st)
            for q in range(4):
                act.wait_ge(S["xt_ps"], 5 + q)
                nc.scalar.activation(ctxT[:, 4 * q:4 * q + 4, :], tiles(mp[q % 2][:, :]), ACT.Copy)\
                    .then_inc(S["ct_sb"], 1)
            act.wait_ge(S["xt_sb"], 4)
            act.wait_ge(S["eps_ok"], 3)
            norm_squares(act, 0, xT)
            act.wait_ge(S["ct_sb"], 4)
            norm_squares(act, 1, ctxT)
            norm_root(act, 0, mp[0])
            norm_root(act, 1, mp[1])
            C = lambda *a, **k: conv_hi(act, *a, **k)
            with act.Fori(0, 3) as g:
                it = st.inside(g, 2, (0, 0))
                for b in range(2):
                    split_ahead(C, it)
            st.passed(3, 2, (0, 0))
            act.wait_ge(S["mod_a"], 1)
            apply_act(act, 0, hh, lambda kt: mpre[:, 0, 1, kt:kt + 1], lambda kt: mpre[:, 0, 0, kt:kt + 1])
            apply_act(act, 1, ch, lambda kt: mpre[:, 1, 1, kt:kt + 1], lambda kt: mpre[:, 1, 0, kt:kt + 1])
            for n, (c0, width, cw) in enumerate(TOKEN):
                split_ahead(C, st, width=width, nwidth=NEXT_W[n])
                if cw:
                    group_done(act, st)
                    src = mp[n % 2][:, :].rearrange("p (t n) -> p t n", t=2)
                    if c0 == C_LR:
                        act.wait_ge(S["spill_ok"], 16)
                        dst = lrn[:, 2:4, :, 0:RANK]
                        src = mp[n % 2][:, :].rearrange("p (t n) -> p t n", t=2)[:, :, 0:cw]\
                            .rearrange("p t (d r) -> p t d r", d=2)
                        for t in range(2):
                            last = nc.scalar.activation(dst[:, t], src[:, t], ACT.Copy)
                    else:
                        dst = ckn[:, :, :] if c0 == C_K else cvn[:, :, c0 - C_V:c0 - C_V + GC]
                        last = nc.scalar.activation(dst, src, ACT.Copy)
                    last.then_inc(acc_free[n % 2], 1)
            a_n = 0
            sts = 0
            for m, (src, d, t) in enumerate(SCANS):
                l = m - 4
                act.wait_ge(S["z_ps"], m + 1)
                if m:
                    act.wait_ge(S["ke_ok"], m)
                nc.scalar.activation(tq[:, 0, :], mp[0][:, GC:2 * GC], ACT.Abs).then_inc(S["a_self"], 1)
                own(a_n + 1)
                nc.scalar.activation(tq[:, 0, :], tq[:, 0, :], ACT.Exp, scale=-1.0).then_inc(S["a_self"], 1)
                own(a_n + 2)
                a_n += 2
                nc.scalar.activation(tq[:, 0, :], tq[:, 0, :], ACT.Ln, bias=1.0).then_inc(S["ln_ok"], 1)
                act.wait_ge(S["cum_ps"], m + 1)
                if sts:
                    act.wait_ge(S["st_ok"], sts)
                nc.scalar.activation(dec[:, :, :].rearrange("p h c -> p (h c)"), mp[0][:, 0:2 * HEADS],
                                     ACT.Exp)
                nc.scalar.activation(tq[:, 1, :], mp[1][:, 0:GC], ACT.Exp).then_inc(S["kexp_ok"], 1)
                if src:
                    nc.scalar.activation(tmp[:, 0, 0:GC], mp[1][:, GC:2 * GC], ACT.Exp)
                    nc.scalar.activation(tmp[:, 0, GC:2 * GC], mp[1][:, GC:2 * GC], ACT.Exp, scale=-1.0)\
                        .then_inc(S["qexp_ok"], 1)
                    act.wait_ge(S["qkT_ps"], l + 1)
                    nc.scalar.activation(kiT[:, :], mp[0][:, GC:2 * GC], ACT.Copy).then_inc(S["qkT_sb"], 1)
                sts += 1 if src and t == (1, 0)[d] else 2
            act.wait_ge(S["o_ok"], 4)
            for t in range(2):
                for h in range(HEADS):
                    n = t * HEADS + h
                    last = nc.scalar.activation(tmp[:, t, h * DV:(h + 1) * DV], osb[:, t, h * DV:(h + 1) * DV],
                                                ACT.Square, accum_out=oss[:, 0, n:n + 1])
            last.then_inc(S["oss_ok"], 1)
            act.wait_ge(S["oss_ok"], 1)
            nc.scalar.activation(oss[:, 1, :], oss[:, 0, :], ACT.Sqrt, bias=eps[:, 0:1], scale=1.0 / DV)\
                .then_inc(S["ort_ok"], 1)
            for g in range(FGROUPS):
                act.wait_ge(S["p_ps"], g + 1)
                if g:
                    act.wait_ge(S["y_ps"], g)
                pv = mp[0][:, :].rearrange("p (t n) -> p t n", t=2)
                nc.scalar.activation(pbuf[:, :, 0:NT], pv[:, :, 0:NT], ACT.Copy)
                nc.scalar.activation(pbuf[:, :, NT:2 * NT], pv[:, :, NT:2 * NT], ACT.Copy, scale=-1.0)\
                    .then_inc(S["p_sb"], 1)
                act.wait_ge(S["y_ps"], g + 1)
                nc.scalar.activation(yfh[:, 2 * g:2 * g + 2, :], tiles(mp[1][:, 0:2 * NT]), ACT.Copy)\
                    .then_inc(S["yhi_ok"], 1)
            for g in range(2):
                split_ahead(C, st)
                group_done(act, st)
                nc.scalar.activation(sg[:, 4 * g:4 * g + 4, :], tiles(acc[(7 + g) % 2][:, :]), ACT.Sigmoid)\
                    .then_inc(S["sg_a"], 1)
            for q in range(2):
                act.wait_ge(S["ot_ok"], q + 1)
                nc.scalar.activation(oh[:, 4 * q:4 * q + 4, :], tiles(tmp[:, q, :]), ACT.Copy)\
                    .then_inc(S["ohi_ok"], 1)
            act.wait_ge(S["olo_ok"], 2)
            with act.Fori(0, 4) as j:
                it = st.inside(j, 3, (0, 0))
                act.wait_ge(S["mlo_ok"], j + 1)
                for i in range(2):
                    split_ahead(C, it)
                    group_done(act, it)
                    nc.scalar.activation(tmp[:, i, :], acc[1 - i][:, :], ACT.Sigmoid)\
                        .then_inc(S["gate_ok"], 1)
                split_ahead(C, it)
                act.wait_ge(S["mt_ok"], j + 2)
                nc.scalar.activation(mh[:, ds(4 * j, 4), :], tiles(tmp[:, 0, :]), ACT.Copy)\
                    .then_inc(S["mhi_ok"], 1)
            st.passed(4, 3, (0, 0))
            with act.Fori(0, 4) as g:
                split_ahead(C, st.inside(g, 1, (0, 0)))
            st.passed(4, 1, (0, 0))
            act.wait_ge(S["mods_ok"], 17)
            act.wait_ge(S["mlo_ok"], 5)
            norm_squares(act, 2, xT2)
            norm_root(act, 2, mp[0])
            act.wait_ge(S["mod_b"], 1)
            apply_act(act, 2, hh, lambda kt: a2[:, kt:kt + 1], lambda kt: mods[:, KT + kt:KT + kt + 1])
            act.wait_ge(S["lo_ok"], 12)
            with act.Fori(0, MLP_CHUNKS) as c:
                it = st.inside(c, 8, (0, 0))
                for g in range(4):
                    n = 4 * c + g
                    split_ahead(C, it)
                    group_done(act, it)
                    nc.scalar.activation(tmp[:, 0, :], acc[g % 2][:, :], ACT.Relu).then_inc(S["relu_ok"], 1)
                    act.wait_ge(S["rsq_ok"], n + 1)
                    nc.scalar.activation(mh[:, 4 * g:4 * g + 4, :], tiles(tmp[:, 1, :]), ACT.Copy)\
                        .then_inc(S["hhi_ok"], 1)
                for g in range(4):
                    split_ahead(C, it)
            st.passed(MLP_CHUNKS, 8, (0, 0))
            all_read(act, F_MLP)
            norm_squares(act, 3, xT2)
            norm_root(act, 3, mp[0])
            act.wait_ge(S["vt_ok"], 4)
            norm_squares(act, 4, xT2)
            norm_root(act, 4, mp[0])
            apply_act(act, 3, hh, lambda kt: pcol("norm_mix_pre_2", kt), None)
            with act.Fori(0, 2) as g:
                it = st.inside(g, 2, (0, 0))
                for b in range(2):
                    split_ahead(C, it)
            st.passed(2, 2, (0, 0))
            all_read(act, F_UB)
            nc.scalar.activation(uT[:, 24:30, :], uT[:, 24:30, :], ACT.Sigmoid).then_inc(S["bsig_ok"], 1)
            with act.Fori(0, 2) as g:
                it = st.inside(g, 2, (0, 0))
                for b in range(2):
                    split_ahead(C, it)
            st.passed(2, 2, (0, 0))
            split_ahead(C, st, width=C2_B - 4 * GC)
            tf = tmp[:, :, :].rearrange("p a n -> p (a n)")
            act.wait_ge(S["a_ok"], 1)
            nc.scalar.activation(mh[:, 0:TA, :], uT[:, 12:12 + TA, :], ACT.Copy).then_inc(S["mxh_ok"], 1)
            act.wait_ge(S["pool_ps"], 1)
            for t in range(TC):
                last = nc.scalar.activation(uT[:, 30 + t, :], mp[0][:, t * NT:(t + 1) * NT], ACT.Copy,
                                            scale=pcol("pool_scale_2", t))
            last.then_inc(S["pool_sb"], 1)
            act.wait_ge(S["pool_sb"], 1)
            nc.scalar.activation(mh[:, TA + TB:KT, :], uT[:, 30:34, :], ACT.Copy).then_inc(S["mxh_ok"], 1)
            act.wait_ge(S["ln_d"], 1)
            nc.scalar.activation(tf[:, 0:WB * 2], uT[:, 24:30, :].rearrange("p t n -> p (t n)"), ACT.Square)\
                .then_inc(S["ln_sq"], 1)
            act.wait_ge(S["ln_ps"], 2)
            nc.scalar.activation(root[:, :], mp[1][:, GC:GC + NT], ACT.Sqrt, bias=eps[:, 1:2], scale=1.0 / WB)\
                .then_inc(S["ln_rt"], 1)
            act.wait_ge(S["ln_d"], 2)
            for t in range(TB):
                last = nc.scalar.activation(uT[:, 24 + t, :], uT[:, 24 + t, :], ACT.Identity,
                                            bias=pcol("ln_b_bias_2", t), scale=pcol("ln_b_gain_2", t))
            last.then_inc(S["ln_z"], 1)
            act.wait_ge(S["ln_z"], 1)
            nc.scalar.activation(tf[:, 0:WB * 2], uT[:, 24:30, :].rearrange("p t n -> p (t n)"), ACT.Sigmoid)\
                .then_inc(S["ln_sg"], 1)
            act.wait_ge(S["ln_d"], 3)
            nc.scalar.activation(mh[:, TA:TA + TB, :], uT[:, 24:30, :], ACT.Copy).then_inc(S["mxh_ok"], 1)
            with act.Fori(0, 4) as g:
                split_ahead(C, st.inside(g, 1, (0, 0)))
            st.passed(4, 1, (0, 0))
            all_read(act, F_OUT2)
            norm_squares(act, 5, yT)
            norm_root(act, 5, mp[0])
            act.wait_ge(S["vt_ok"], 8)
            norm_squares(act, 6, xT2)
            norm_root(act, 6, mp[0])
            apply_act(act, 4, hh, lambda kt: pcol("norm_ffn_pre_2", kt), None)
            act.wait_ge(S["lo_ok"], 20)

            def ffn_pair(it, c, p, n, **kw):
                for v in range(2):
                    split_ahead(C, it, **(kw if v else {}))
                    group_done(act, it)
                    up = (up1, up2)[v]
                    for t in range(4):
                        col = 16 * c + 4 * p + t + FT * v
                        last = nc.scalar.activation(
                            up[:, t, :], acc[v][:, t * NT:(t + 1) * NT], ACT.Identity,
                            bias=par[:, ds(COL["conv_ffn_bias_2"] + col, 1)],
                            scale=par[:, ds(COL["conv_ffn_w_2"] + 4 * FT + col, 1)])
                    last.then_inc(S["ct_ok"], 1)
                    act.wait_ge(S["cd_ok"], 2 * n + v + 1)
                    if v == 0:
                        nc.scalar.activation(tiles(tmp[:, 0, :]), up1[:, :, :], ACT.Sigmoid)\
                            .then_inc(S["gs_ok"], 1)
                    else:
                        act.wait_ge(S["gm_ok"], n + 1)
                        nc.scalar.activation(mh[:, 4 * p:4 * p + 4, :], tiles(tmp[:, 1, :]), ACT.Copy)\
                            .then_inc(S["fhi_ok"], 1)
            with act.Fori(0, 2) as c:
                it = st.inside(c, 12, (0, 0))
                for p in range(4):
                    ffn_pair(it, c, p, 4 * c + p)
                for g in range(4):
                    split_ahead(C, it)
            st.passed(2, 12, (0, 0))
            for p in range(3):
                ffn_pair(st, 2, p, 8 + p)
            for g in range(4):
                split_ahead(C, st, slots=3, last=g == 3, after3=True)
            all_read(act, F_FFN)
            norm_squares(act, 7, yT)
            norm_root(act, 7, mp[0])

        @block.vector
        def _(dve):
            st = Turns()
            seen = [0]

            def own(ins):
                ins.then_inc(S["v_self"], 1)
                seen[0] += 1
                dve.wait_ge(S["v_self"], seen[0])

            for name in ("red_ps", "mods_ok", "mt_ok", "mlo_ok", "tap_ok"):
                dve.sem_inc(S[name], 1)
            nc.vector.memset(ones[:, :], 1.0).then_inc(S["eps_ok"], 1)
            nc.vector.memset(eps[:, 0:1], EPS).then_inc(S["eps_ok"], 1)
            nc.vector.memset(eps[:, 1:2], LN_EPS).then_inc(S["eps_ok"], 1)
            dve.wait_ge(S["par_ps"], 1)
            nc.vector.tensor_copy(par[:, :], mp[1][:, 0:NPARAM]).then_inc(S["par_sb"], 1)
            dve.wait_ge(S["par_sb"], 1)
            dve.wait_ge(S["csig_ok"], 1)
            nc.vector.tensor_tensor(csil[:, :, :], pcol("c", 0, 2 * KT).rearrange("p (v k) -> p v k", v=2),
                                    csig[:, :, :], ALU.mult).then_inc(S["csil_ok"], 1)
            dve.wait_ge(S["csil_ok"], 1)
            dve.wait_ge(S["chi_ok"], 1)
            nc.vector.tensor_tensor(cv[:, :, 2:4], csil[:, :, :].rearrange("p v k -> p k v"),
                                    cv[:, :, 0:2].bitcast(f32), ALU.subtract).then_inc(S["cv_ok"], 1)
            C = lambda *a, **k: conv_lo(dve, *a, **k)

            def mod_evac(it, g, i):
                split_ahead(C, it)
                group_done(dve, it)
                nc.vector.tensor_copy(mraw[:, ds(4 * g, 4), :],
                                      acc[i][:, 0:16].rearrange("p (t v) -> p t v", v=4))\
                    .then_inc(acc_free[i], 1)
            conv_lo(dve, st, (0, 1))
            for g in range(2):
                mod_evac(st, g, g)
            dve.wait_ge(S["x_in"], 32)
            for q in range(4):
                dve.wait_ge(S["xt_ps"], q + 1)
                nc.vector.tensor_tensor(xT[:, 4 * q:4 * q + 4, :], tiles(mp[q % 2][:, :]),
                                        posT[:, 4 * q:4 * q + 4, :], ALU.add).then_inc(S["xt_sb"], 1)
            norm_rstd(dve, 0)
            norm_rstd(dve, 1)
            with dve.Fori(0, 3) as g:
                it = st.inside(g, 2, (0, 0))
                for b in range(2):
                    mod_evac(it, 2 * g + 2 + b, b)
            st.passed(3, 2, (0, 0))
            all_read(dve, (4, 4))
            own(nc.vector.tensor_tensor(msum[:, :, :], mraw[:, :, 0:2], mraw[:, :, 2:4], ALU.add))
            for v in range(2):
                own(nc.vector.tensor_tensor(mpre[:, v, :, :].rearrange("p a k -> p (a k)"),
                                            msum[:, :, v:v + 1].rearrange("p n a -> p (n a)"),
                                            pcol("b_mod", 0, 2 * KT), ALU.add))
            for v in range(2):
                last = nc.vector.scalar_tensor_tensor(mpre[:, v, 1, :], mpre[:, v, 1, :], 1.0,
                                                      pcol("norm1_g", 0, KT), ALU.add, ALU.mult)
            last.then_inc(S["mod_a"], 1)
            apply_dve(dve, 0, 0, xT, hl, hh)
            apply_dve(dve, 1, 1, ctxT, cl, ch)

            dve.wait_ge(S["spill_ok"], 16)
            nc.vector.memset(lrn[:, :, :, RANK:RANK + 1], 1.0)
            for n, (c0, width, cw) in enumerate(TOKEN):
                split_ahead(C, st, width=width, nwidth=NEXT_W[n])
                group_done(dve, st)
                src = acc[n % 2][:, :].rearrange("p (t n) -> p t n", t=2)
                if c0 == C_K:
                    last = nc.vector.tensor_copy(kn[:, :, :], src)
                elif c0 == C_Q:
                    last = nc.vector.tensor_scalar(qn[:, :, :], src, float(DK) ** -0.5, None, ALU.mult)
                elif c0 < C_GOUT:
                    last = nc.vector.tensor_copy(vn[:, :, c0 - C_V:c0 - C_V + GC], src)
                elif c0 == C_LR:
                    for t in range(2):
                        nc.vector.tensor_copy(lrn[:, t, :, 0:RANK],
                                              src[:, t, 0:cw].rearrange("p (d r) -> p d r", d=2))
                    last = nc.vector.tensor_copy(un[:, :, 0:GC - cw], src[:, :, cw:GC])
                else:
                    u0 = c0 - C_U
                    last = nc.vector.tensor_copy(un[:, :, u0:u0 + width], src[:, :, 0:width])
                last.then_inc(acc_free[n % 2], 1)
            dve.wait_ge(S["spill_ok"], 16)
            nc.vector.memset(sT[:, :, :], 0.0).then_inc(S["nat_v"], 4)
            for m, (src, d, t) in enumerate(SCANS):
                l = m - 4
                dve.wait_ge(S["lrT_ps"], m + 1)
                nc.vector.tensor_copy(lrT[:, :], mp[0][0:RANK + 1, 0:P]).then_inc(S["lrT_sb"], 1)
                dve.wait_ge(S["ln_ok"], m + 1)
                nc.vector.scalar_tensor_tensor(lab[:, m % 2, :], mp[0][:, GC:2 * GC], 0.0, tq[:, 0, :],
                                               ALU.min, ALU.subtract).then_inc(S["la_ok"], 1)
                dve.wait_ge(S["kexp_ok"], m + 1)
                nc.vector.tensor_tensor(keb[:, m % 2, :], (kn if src else ckn)[:, t, :], tq[:, 1, :],
                                        ALU.mult).then_inc(S["ke_ok"], 1)
                if src:
                    dve.wait_ge(S["qexp_ok"], l + 1)
                    nc.vector.tensor_tensor(tmp[:, 1, 0:GC], qn[:, t, :], tmp[:, 0, 0:GC], ALU.mult)
                    nc.vector.tensor_tensor(tmp[:, 1, GC:2 * GC], kn[:, t, :], tmp[:, 0, GC:2 * GC],
                                            ALU.mult).then_inc(S["qk_ok"], 1)
                    dve.wait_ge(S["qkT_ps"], l + 1)
                    nc.vector.tensor_copy(qdT[:, :], mp[0][:, 0:GC]).then_inc(S["qkT_sb"], 1)
                    dve.wait_ge(S["sc_ps"], l + 1)
                    nc.vector.copy_predicated(
                        sT[:, d, :].rearrange("p (h n) -> p h n", h=HEADS),
                        cum_w[d].bitcast(u32).rearrange("p (a n) -> p a n", a=1).to_broadcast([P, HEADS, P]),
                        mp[1][:, 0:GC].rearrange("p (h n) -> p h n", h=HEADS)).then_inc(S["sc_sb"], 1)
                for ci in range(2):
                    dve.wait_ge(S["u_ps"], 2 * m + ci + 1)
                    if src and t == (1, 0)[d] and ci == 1:
                        break
                    half = (ci, 1 - ci)[d]
                    if not src and t == (0, 1)[d] and ci == 0:
                        nc.vector.tensor_copy(state[:, d, :, :].rearrange("p h n -> p (h n)"), mp[1][:, :])\
                            .then_inc(S["st_ok"], 1)
                        continue
                    for h in range(HEADS):
                        last = nc.vector.scalar_tensor_tensor(
                            state[:, d, h, :], state[:, d, h, :], dec[:, h, half:half + 1],
                            mp[1][:, h * DV:(h + 1) * DV], ALU.mult, ALU.add)
                    last.then_inc(S["st_ok"], 1)
                if src:
                    if d == 0:
                        nc.vector.tensor_copy(osb[:, t, :], mp[0][:, :]).then_inc(S["o_ok"], 1)
                    else:
                        nc.vector.tensor_tensor(osb[:, t, :], mp[0][:, :], osb[:, t, :], ALU.add)\
                            .then_inc(S["o_ok"], 1)
            dve.wait_ge(S["ort_ok"], 1)
            own(nc.vector.reciprocal(oss[:, 0, :], oss[:, 1, :]))
            for t in range(2):
                for h in range(HEADS):
                    n = t * HEADS + h
                    part = osb[:, t, h * DV:(h + 1) * DV]
                    last = nc.vector.tensor_scalar(part, part, oss[:, 0, n:n + 1], None, ALU.mult)
            last.then_inc(S["ons_ok"], 1)
            for g in range(FGROUPS):
                dve.wait_ge(S["yhi_ok"], g + 1)
                nc.vector.tensor_tensor(yfl[:, 2 * g:2 * g + 2, :], tiles(mp[1][:, 0:2 * NT]),
                                        yfh[:, 2 * g:2 * g + 2, :].bitcast(f32), ALU.subtract)\
                    .then_inc(S["ylo_ok"], 1)
            for g in range(2):
                split_ahead(C, st)
                group_done(dve, st)
                i = (7 + g) % 2
                dve.wait_ge(S["sg_a"], g + 1)
                nc.vector.tensor_tensor(sg[:, 4 * g:4 * g + 4, :], tiles(acc[i][:, :]),
                                        sg[:, 4 * g:4 * g + 4, :], ALU.mult).then_inc(S["sg_v"], 1)
            dve.wait_ge(S["sg_v"], 2)
            for q in range(2):
                dve.wait_ge(S["oT_ps"], q + 1)
                for t in range(4):
                    i = 4 * q + t
                    last = nc.vector.scalar_tensor_tensor(
                        tmp[:, q, t * NT:(t + 1) * NT], mp[q][:, t * NT:(t + 1) * NT],
                        pcol("gla_norm_g", i % 2), sg[:, i, :], ALU.mult, ALU.mult)
                last.then_inc(S["ot_ok"], 1)
            for q in range(2):
                dve.wait_ge(S["ohi_ok"], q + 1)
                nc.vector.tensor_tensor(ol[:, 4 * q:4 * q + 4, :], tiles(tmp[:, q, :]),
                                        oh[:, 4 * q:4 * q + 4, :].bitcast(f32), ALU.subtract)\
                    .then_inc(S["olo_ok"], 1)

            def mac(w):
                seen_pieces = [0]

                def add(_):
                    p = seen_pieces[0]
                    seen_pieces[0] += 1
                    if p == 0:
                        dve.wait_ge(S["red_ps"], w + 1)
                    dve.wait_ge(wm_in[p % 2], 64 * w + 16 * (p // 2) + 16)
                    for k in range(2):
                        kt = 2 * p + k
                        if kt == 0:
                            nc.vector.tensor_scalar(wacc[:, :], wmr[:, 0, 0, :], csil[:, 0, 0:1], None,
                                                    ALU.mult).then_inc(S["mac_ok"], 1)
                        else:
                            dve.wait_ge(S["mac_ok"], 16 * w + kt)
                            nc.vector.scalar_tensor_tensor(
                                wacc[:, :], wmr[:, p % 2, k, :], csil[:, 0, kt:kt + 1], wacc[:, :],
                                ALU.mult, ALU.add).then_inc(S["mac_ok"], 1)
                return add

            def mods_out(w):
                dve.wait_ge(S["red_ps"], w + 2)
                nc.vector.tensor_tensor(mods[:, ds(4 * w, 4)], mp[1][:, 0:4],
                                        par[:, ds(COL["b_mod"] + 2 * KT + 4 * w, 4)], ALU.add)\
                    .then_inc(S["mods_ok"], 1)

            with dve.Fori(0, 4) as j:
                it = st.inside(j, 3, (0, 0))
                for i in range(2):
                    split_ahead(C, it, mac=mac(3 * j + i))
                    mods_out(3 * j + i)
                split_ahead(C, it, mac=mac(3 * j + 2))
                group_done(dve, it)
                dve.wait_ge(S["gate_ok"], 2 * j + 2)
                for i in range(2):
                    nc.vector.tensor_tensor(tmp[:, i, :], acc[1 - i][:, :], tmp[:, i, :], ALU.mult)\
                        .then_inc(S["mrg_ok"], 1)
                dve.wait_ge(S["mrg_ok"], 2 * j + 2)
                nc.vector.tensor_tensor(tmp[:, 0, :], tmp[:, 0, :], tmp[:, 1, :], ALU.add)\
                    .then_inc(S["mt_ok"], 1)
                dve.wait_ge(S["mhi_ok"], j + 1)
                nc.vector.tensor_tensor(ml[:, ds(4 * j, 4), :], tiles(tmp[:, 0, :]),
                                        mh[:, ds(4 * j, 4), :].bitcast(f32), ALU.subtract)\
                    .then_inc(S["mlo_ok"], 1)
                mods_out(3 * j + 2)
            st.passed(4, 3, (0, 0))

            def add_scaled(i, base, gate):
                for t in range(4):
                    x = xT2[:, ds(base + t, 1), :].rearrange("p a n -> p (a n)")
                    last = nc.vector.scalar_tensor_tensor(x, acc[i][:, t * NT:(t + 1) * NT],
                                                          mods[:, ds(gate + base + t, 1)], x,
                                                          ALU.mult, ALU.add)
                return last
            dve.wait_ge(S["x_back"], 16)
            with dve.Fori(0, 2) as g:
                it = st.inside(g, 2, (0, 0))
                for b in range(2):
                    split_ahead(C, it, mac=mac(12 + 2 * g + b))
                    group_done(dve, it)
                    add_scaled(1 - b, 8 * g + 4 * b, 0).then_inc(acc_free[1 - b], 1)
                    mods_out(12 + 2 * g + b)
            st.passed(2, 2, (0, 0))
            dve.wait_ge(S["mods_ok"], 17)
            nc.vector.scalar_tensor_tensor(a2[:, :], mods[:, 2 * KT:3 * KT], 1.0, pcol("norm2_g", 0, KT),
                                           ALU.add, ALU.mult).then_inc(S["mod_b"], 1)
            norm_rstd(dve, 2)
            apply_dve(dve, 2, 2, xT2, hl, hh)
            with dve.Fori(0, MLP_CHUNKS) as c:
                it = st.inside(c, 8, (0, 0))
                for g in range(4):
                    n = 4 * c + g
                    split_ahead(C, it)
                    group_done(dve, it)
                    dve.wait_ge(S["relu_ok"], n + 1)
                    nc.vector.scalar_tensor_tensor(tmp[:, 1, :], acc[g % 2][:, :], 0.0, tmp[:, 0, :],
                                                   ALU.max, ALU.mult).then_inc(S["rsq_ok"], 1)
                    dve.wait_ge(S["hhi_ok"], n + 1)
                    nc.vector.tensor_tensor(ml[:, 4 * g:4 * g + 4, :], tiles(tmp[:, 1, :]),
                                            mh[:, 4 * g:4 * g + 4, :].bitcast(f32), ALU.subtract)\
                        .then_inc(S["hid_ok"], 1)
                for g in range(4):
                    split_ahead(C, it)
                    group_done(dve, it)
                    add_scaled(g % 2, 4 * g, 3 * KT).then_inc(acc_free[g % 2], 1)
            st.passed(MLP_CHUNKS, 8, (0, 0))
            norm_rstd(dve, 3)
            dve.wait_ge(S["rs_ok"], 4)
            dve.wait_ge(S["ms_ok"], 16)
            for q in range(4):
                own(nc.vector.tensor_tensor(tiles(tmp[:, q % 2, :]), xT2[:, 4 * q:4 * q + 4, :], rbc(3),
                                            ALU.mult))
                for t in range(4):
                    last = nc.vector.tensor_scalar(xT2[:, 4 * q + t, :], tmp[:, q % 2, t * NT:(t + 1) * NT],
                                                   pcol("final_norm_g", 4 * q + t), None, ALU.mult)
                last.then_inc(S["vt_ok"], 1)
            norm_rstd(dve, 4)
            apply_dve(dve, 3, 4, xT2, hl, hh)
            with dve.Fori(0, 2) as g:
                it = st.inside(g, 2, (0, 0))
                for b in range(2):
                    split_ahead(C, it)
                    group_done(dve, it)
                    nc.vector.tensor_copy(uT[:, ds(3 * TA + 8 * g + 4 * b, 4), :], tiles(acc[b][:, :]))\
                        .then_inc(acc_free[b], 1)
            st.passed(2, 2, (0, 0))
            dve.wait_ge(S["bsig_ok"], 1)
            own(nc.vector.tensor_tensor(uT[:, 18:24, :], uT[:, 18:24, :], uT[:, 24:30, :], ALU.mult))

            def tap(i, sh):
                def tile(t):
                    return uT[:, ds(t + i, 1), :].rearrange("p a n -> p (a n)")
                x, done = tile(18), (KCONV + 1) * i
                if sh == KCONV:
                    dve.wait_ge(S["tap_ok"], done + KCONV + 1)
                    ins = nc.vector.tensor_tensor(tile(24), cacc[:, 0, :], cacc[:, 1, :], ALU.add)
                else:
                    dve.wait_ge(S["tap_ok"], done + max(sh, 1))
                    w = par[:, ds(COL["conv_b_w_2"] + TB * (KCONV - 1 - sh) + i, 1)]
                    part = cacc[:, sh % 2, sh:NT]
                    if sh == 0:
                        ins = nc.vector.tensor_scalar(part, x, w, par[:, ds(COL["conv_b_bias_2"] + i, 1)],
                                                      ALU.mult, ALU.add)
                    elif sh == 1:
                        nc.vector.memset(cacc[:, 1, 0:1], 0.0)
                        ins = nc.vector.tensor_scalar(part, x[:, 0:NT - 1], w, None, ALU.mult)
                    else:
                        ins = nc.vector.scalar_tensor_tensor(part, x[:, 0:NT - sh], w, part, ALU.mult, ALU.add)
                ins.then_inc(S["tap_ok"], 1)

            def taps(g, n0):
                piece = [0]

                def add(_):
                    for n in range(n0 + 6 * piece[0], n0 + 6 * piece[0] + 6):
                        tap(3 * g + n // (KCONV + 1), n % (KCONV + 1))
                    piece[0] += 1
                return add
            with dve.Fori(0, 2) as g:
                it = st.inside(g, 2, (0, 0))
                for b in range(2):
                    split_ahead(C, it, mac=taps(g, 48 * b))
                    group_done(dve, it)
                    nc.vector.tensor_copy(uT[:, ds(8 * g + 4 * b, 4), :], tiles(acc[b][:, :]))\
                        .then_inc(acc_free[b], 1)
            st.passed(2, 2, (0, 0))
            split_ahead(C, st, width=C2_B - 4 * GC)
            group_done(dve, st)
            nc.vector.tensor_copy(uT[:, 16:18, :], tiles(acc[0][:, 0:2 * NT]))\
                .then_inc(acc_free[0], 1)
            all_read(dve, F_U)
            own(nc.vector.tensor_tensor(uT[:, 6:12, :], uT[:, 6:12, :], uT[:, 12:18, :], ALU.mult))
            for sh in range(3):
                for t in range(TA):
                    w = pcol("conv_a_w_2", TA * (2 - sh) + t)
                    x, y = uT[:, 6 + t, 0:NT - sh], uT[:, 12 + t, sh:NT]
                    if sh == 0:
                        last = nc.vector.tensor_scalar(y, x, w, None, ALU.mult)
                    else:
                        last = nc.vector.scalar_tensor_tensor(y, x, w, y, ALU.mult, ALU.add)
                own(last)
            nc.vector.tensor_tensor(uT[:, 12:18, :], uT[:, 12:18, :], uT[:, 0:6, :], ALU.mult)\
                .then_inc(S["a_ok"], 1)
            dve.wait_ge(S["ln_ps"], 1)
            own(nc.vector.tensor_scalar(root[:, :], mp[1][:, 0:NT], 1.0 / WB, None, ALU.mult))
            nc.vector.tensor_tensor(uT[:, 24:30, :], uT[:, 24:30, :],
                                    root[:, :].rearrange("p (a n) -> p a n", a=1).to_broadcast([P, TB, NT]),
                                    ALU.subtract).then_inc(S["ln_d"], 1)
            pa, pb = tiles(tmp[:, 0, :]), tiles(tmp[:, 1, :])
            src, dst = uT[:, 30:34, :], pa
            for g in range(TC):
                sh = 1 << g
                nc.vector.tensor_copy(dst[:, g:4, 0:sh], src[:, g:4, 0:sh])
                own(nc.vector.tensor_tensor(dst[:, g:4, sh:NT], src[:, g:4, sh:NT], src[:, g:4, 0:NT - sh],
                                            ALU.add))
                part = dst[:, g, :]
                own(nc.vector.tensor_tensor(part[:, 0:16], part[:, 0:16], fix_w[:, g, :], ALU.mult)
                    if g == 3 else
                    nc.vector.tensor_tensor(fixed[:, g, :], part[:, 0:16], fix_w[:, g, :], ALU.mult))
                src, dst = dst, (pb, pa)[(g + 1) % 2 == 0]
            for g in range(TC):
                w = 2 << g
                part = (pa, pb)[g % 2][:, g, :]
                x = uT[:, 30 + g, :]
                if g < 3:
                    nc.vector.scalar_tensor_tensor(x[:, 0:16], fixed[:, g, :], 1.0 / w, x[:, 0:16],
                                                   ALU.mult, ALU.subtract)
                    last = nc.vector.scalar_tensor_tensor(x[:, 16:NT], part[:, 16:NT], 1.0 / w, x[:, 16:NT],
                                                          ALU.mult, ALU.subtract)
                else:
                    last = nc.vector.scalar_tensor_tensor(x, part, 1.0 / w, x, ALU.mult, ALU.subtract)
            last.then_inc(S["pooled_ok"], 1)
            dve.wait_ge(S["mxh_ok"], 1)
            nc.vector.tensor_tensor(ml[:, 0:TA, :], uT[:, 12:18, :], mh[:, 0:TA, :].bitcast(f32),
                                    ALU.subtract).then_inc(S["mxl_ok"], 1)
            dve.wait_ge(S["mxh_ok"], 2)
            nc.vector.tensor_tensor(ml[:, 12:16, :], uT[:, 30:34, :], mh[:, 12:16, :].bitcast(f32),
                                    ALU.subtract).then_inc(S["mxl_ok"], 1)
            dve.wait_ge(S["ln_rt"], 1)
            own(nc.vector.reciprocal(rstd[:, 1, :], root[:, :]))
            nc.vector.tensor_tensor(uT[:, 24:30, :], uT[:, 24:30, :], rbc(1, TB), ALU.mult)\
                .then_inc(S["ln_d"], 1)
            dve.wait_ge(S["ln_sg"], 1)
            nc.vector.tensor_tensor(uT[:, 24:30, :], uT[:, 24:30, :],
                                    tmp[:, :, :].rearrange("p a n -> p (a n)")[:, 0:2 * WB]
                                    .rearrange("p (t n) -> p t n", n=NT), ALU.mult).then_inc(S["ln_d"], 1)
            dve.wait_ge(S["mxh_ok"], 3)
            nc.vector.tensor_tensor(ml[:, 6:12, :], uT[:, 24:30, :], mh[:, 6:12, :].bitcast(f32),
                                    ALU.subtract).then_inc(S["mxl_ok"], 1)
            with dve.Fori(0, 2) as g:
                it = st.inside(g, 2, (0, 0))
                for b in range(2):
                    split_ahead(C, it)
                    group_done(dve, it)
                    nc.vector.tensor_copy(yT[:, ds(8 * g + 4 * b, 4), :], tiles(acc[1 - b][:, :]))\
                        .then_inc(acc_free[1 - b], 1)
            st.passed(2, 2, (0, 0))

            def norm_add(k, name, sem_ok):
                norm_rstd(dve, k)
                dve.wait_ge(S["rs_ok"], k + 1)
                for q in range(4):
                    own(nc.vector.tensor_tensor(tiles(tmp[:, q % 2, :]), yT[:, 4 * q:4 * q + 4, :], rbc(k),
                                                ALU.mult))
                    for t in range(4):
                        x = xT2[:, 4 * q + t, :]
                        last = nc.vector.scalar_tensor_tensor(x, tmp[:, q % 2, t * NT:(t + 1) * NT],
                                                              pcol(name, 4 * q + t), x, ALU.mult, ALU.add)
                    last.then_inc(sem_ok, 1)
            norm_add(5, "norm_mix_post_2", S["vt_ok"])
            own(nc.vector.memset(yT[:, :, :], 0.0))
            norm_rstd(dve, 6)
            apply_dve(dve, 4, 6, xT2, hl, hh)

            def ffn_pair(it, c, p, n):
                for v in range(2):
                    split_ahead(C, it)
                    group_done(dve, it)
                    up = (up1, up2)[v]
                    dve.wait_ge(S["ct_ok"], 2 * n + v + 1)
                    for sh in (1, 2):
                        for t in range(4):
                            col = COL["conv_ffn_w_2"] + 2 * FT * (2 - sh) + 16 * c + 4 * p + t + FT * v
                            y = up[:, t, sh:NT]
                            last = nc.vector.scalar_tensor_tensor(
                                y, acc[v][:, t * NT:(t + 1) * NT - sh], par[:, ds(col, 1)], y,
                                ALU.mult, ALU.add)
                        if sh == 1:
                            last.then_inc(S["tap2_ok"], 1)
                            dve.wait_ge(S["tap2_ok"], 2 * n + v + 1)
                    last.then_inc(S["cd_ok"], 1)
                    if v == 0:
                        dve.wait_ge(S["gs_ok"], n + 1)
                        nc.vector.tensor_tensor(up1[:, :, :], up1[:, :, :], tiles(tmp[:, 0, :]), ALU.mult)\
                            .then_inc(S["gu_ok"], 1)
                    else:
                        dve.wait_ge(S["gu_ok"], n + 1)
                        dve.wait_ge(S["cd_ok"], 2 * n + 2)
                        nc.vector.tensor_tensor(tiles(tmp[:, 1, :]), up1[:, :, :], up2[:, :, :], ALU.mult)\
                            .then_inc(S["gm_ok"], 1)
                        dve.wait_ge(S["fhi_ok"], n + 1)
                        nc.vector.tensor_tensor(ml[:, 4 * p:4 * p + 4, :], tiles(tmp[:, 1, :]),
                                                mh[:, 4 * p:4 * p + 4, :].bitcast(f32), ALU.subtract)\
                            .then_inc(S["fid_ok"], 1)

            def down_add(g, n):
                y = yT[:, 4 * g:4 * g + 4, :]
                nc.vector.tensor_tensor(y, tiles(acc[g % 2][:, :]), y, ALU.add)\
                    .then_inc(acc_free[g % 2], 1)
            with dve.Fori(0, 2) as c:
                it = st.inside(c, 12, (0, 0))
                for p in range(4):
                    ffn_pair(it, c, p, 4 * c + p)
                for g in range(4):
                    split_ahead(C, it)
                    group_done(dve, it)
                    down_add(g, 4 * c + g)
            st.passed(2, 12, (0, 0))
            for p in range(3):
                ffn_pair(st, 2, p, 8 + p)
            for g in range(4):
                split_ahead(C, st, slots=3, last=g == 3)
                group_done(dve, st, slots=3)
                down_add(g, 8 + g)
            all_read(dve, F_FFN)
            norm_add(7, "norm_ffn_post_2", S["vt_ok"])
            for q in range(4):
                dve.wait_ge(S["out_ps"], q + 1)
                nc.vector.tensor_copy(outn[:, :, 4 * q * P:(4 * q + 4) * P],
                                      mp[q % 2][:, :].rearrange("p (t n) -> p t n", t=2))\
                    .then_inc(S["out_sb"], 1)

        @block.tensor
        def _(pe):
            st = Turns()
            pe.wait_ge(S["con_in"], 16)
            pe.wait_ge(S["par_in"], 16 * NPDMA)
            rows = tmp[:, 0, 0:NPB * P].rearrange("p (b n) -> p b n", b=NPB)
            for b in range(NPB):
                n = min(P, NPARAM - b * P)
                last = nc.tensor.transpose(mp[1][:, b * P:b * P + n], rows[0:n, b, :], ident[0:n, 0:n])
            last.then_inc(S["par_ps"], 1)

            def mm_mod(it, i):
                if not (isinstance(it.f[i], int) and it.f[i] == 0):
                    pe.wait_ge(acc_free[i], it.f[i])
                for s in range(4):
                    for j in range(2):
                        r = (2 * s + j) % 4
                        pe.wait_ge(lo_done[s], 2 * it.u[s] + j + 1)
                        for k in range(2):
                            kt = 4 * s + 2 * j + k
                            for t in range(4):
                                cols = slice(t * P, (t + 1) * P)
                                nc.tensor.matmul(acc[i][:, 4 * t:4 * t + 4], whi[:, r, k, cols], cv[:, kt, :],
                                                 start=kt + t == 0, stop=False, skip_group_check=True)
                                last = nc.tensor.matmul(acc[i][:, 4 * t:4 * t + 2], wlo[:, r, k, cols],
                                                        cv[:, kt, 0:2], start=False, stop=kt == KT - 1,
                                                        skip_group_check=True)
                        last.then_inc(used[s], 1)
                    it.u[s] = it.u[s] + 1
                it.f[i] = it.f[i] + 1
            pe.wait_ge(S["cv_ok"], 1)
            for g in range(2):
                mm_mod(st, g)
            for n in range(8):
                q = n % 4
                if n == 0:
                    pe.wait_ge(S["x_in"], 32)
                    pe.wait_ge(S["par_sb"], 1)
                if n == 4:
                    pe.wait_ge(S["ctx_in"], 16)
                if n >= 2:
                    pe.wait_ge(S["xt_sb"], min(n - 1, 4))
                if n >= 6:
                    pe.wait_ge(S["ct_sb"], n - 5)
                src = stage_c if n >= 4 else stage_x
                for f in range(4):
                    for t in range(2):
                        last = nc.tensor.transpose(mp[n % 2][:, f * NT + t * P:f * NT + (t + 1) * P],
                                                   src[:, t, (4 * q + f) * P:(4 * q + f + 1) * P], ident)
                last.then_inc(S["xt_ps"], 1)
            pe.wait_ge(S["eps_ok"], 3)
            pe.wait_ge(S["ct_sb"], 4)
            norm_sums(pe, 0, mp[0])
            norm_sums(pe, 1, mp[1])
            with pe.Fori(0, 3) as g:
                it = st.inside(g, 2, (1, 1))
                for b in range(2):
                    mm_mod(it, b)
            st.passed(3, 2, (1, 1))
            for n, (c0, width, cw) in enumerate(TOKEN):
                mm_token(pe, st, n % 2, width, cw, ready=h_ready(pe, 0, 2) if n == 0 else None)
            pe.wait_ge(S["gla_in"], 96)
            pe.wait_ge(S["nat_v"], 4)
            pe.wait_ge(acc_free[1], st.f[1])
            pe.wait_ge(acc_free[0], st.f[0])
            stc = 0
            for m, (src, d, t) in enumerate(SCANS):
                l = m - 4
                if m >= 5:
                    pe.wait_ge(S["o_ok"], l)
                elif m:
                    pe.wait_ge(S["kexp_ok"], m)
                nc.tensor.transpose(mp[0][0:RANK + 1, 0:P], lrn[:, (t if src else 2 + t), d, 0:RANK + 1], ident)\
                    .then_inc(S["lrT_ps"], 1)
                pe.wait_ge(S["lrT_sb"], m + 1)
                nc.tensor.matmul(mp[0][:, GC:2 * GC], lrT[:, :], wlr[:, d, :], start=True, stop=True)\
                    .then_inc(S["z_ps"], 1)
                pe.wait_ge(S["la_ok"], m + 1)
                if stc:
                    pe.wait_ge(S["st_ok"], stc)
                la = lab[:, m % 2, :]
                nc.tensor.matmul(mp[1][:, 0:GC], end_w[d], la, start=True, stop=True)
                if src:
                    nc.tensor.matmul(mp[1][:, GC:2 * GC], cum_w[d], la, start=True, stop=True)
                for h in range(HEADS):
                    last = nc.tensor.matmul(mp[0][:, 2 * h:2 * h + 2], la[:, h * DK:(h + 1) * DK], half_w,
                                            start=True, stop=True)
                last.then_inc(S["cum_ps"], 1)
                pe.wait_ge(S["ke_ok"], m + 1)
                v = vn if src else cvn
                if src:
                    pe.wait_ge(S["qk_ok"], l + 1)
                    for x in range(2):
                        for h in range(HEADS):
                            last = nc.tensor.transpose(mp[0][:, x * GC + h * P:x * GC + (h + 1) * P],
                                                       tmp[:, 1, x * GC + h * P:x * GC + (h + 1) * P], ident)
                    last.then_inc(S["qkT_ps"], 1)
                    pe.wait_ge(S["qkT_sb"], 2 * l + 2)
                    for h in range(HEADS):
                        cols = slice(h * P, (h + 1) * P)
                        last = nc.tensor.matmul(mp[1][:, cols], kiT[:, cols], qdT[:, cols],
                                                start=True, stop=True)
                    last.then_inc(S["sc_ps"], 1)
                    pe.wait_ge(S["sc_sb"], l + 1)
                    for h in range(HEADS):
                        nc.tensor.matmul(mp[0][:, h * DV:(h + 1) * DV], sT[:, d, h * P:(h + 1) * P],
                                         v[:, t, h * DV:(h + 1) * DV], start=h % 2 == 0, stop=False,
                                         skip_group_check=True)
                for ci in range(2):
                    half = (ci, 1 - ci)[d]
                    rows = slice(half * CHUNK, (half + 1) * CHUNK)
                    if stc:
                        pe.wait_ge(S["st_ok"], stc)
                    if src:
                        for h in range(HEADS):
                            last = nc.tensor.matmul(mp[0][rows, h * DV:(h + 1) * DV],
                                                    qdT[:, h * P + half * CHUNK:h * P + (half + 1) * CHUNK],
                                                    state[:, d, h, :], start=False, stop=True,
                                                    skip_group_check=True)
                    if not (src and t == (1, 0)[d] and ci == 1):
                        for h in range(HEADS):
                            last = nc.tensor.matmul(mp[1][:, h * DV:(h + 1) * DV],
                                                    keb[rows, m % 2, h * DK:(h + 1) * DK],
                                                    v[rows, t, h * DV:(h + 1) * DV], start=h % 2 == 0,
                                                    stop=True, skip_group_check=True)
                        stc += 1
                    last.then_inc(S["u_ps"], 1)
            for g in range(FGROUPS):
                if g:
                    pe.wait_ge(S["p_sb"], g)
                else:
                    pe.wait_ge(S["o_ok"], 4)
                for dt in range(2):
                    c0 = g * FDIM + dt * P
                    for t in range(2):
                        last = nc.tensor.matmul(mp[0][:, dt * GC:(dt + 1) * GC], un[:, t, c0:c0 + P],
                                                dft[:, t, :], start=t == 0, stop=t == 1)
                last.then_inc(S["p_ps"], 1)
                pe.wait_ge(S["p_sb"], g + 1)
                if g:
                    pe.wait_ge(S["ylo_ok"], g)
                for dt in range(2):
                    for part in range(2):
                        for t in range(2):
                            c0 = part * NT + dt * P
                            last = nc.tensor.matmul(mp[1][:, dt * NT:(dt + 1) * NT], dft[:, t, c0:c0 + P],
                                                    pbuf[:, t, part * NT:(part + 1) * NT],
                                                    start=part + t == 0, stop=part + t == 2)
                last.then_inc(S["y_ps"], 1)
            for g in range(2):
                mm_feature(pe, st, (7 + g) % 2, hh, hl, 0)
            pe.wait_ge(S["ons_ok"], 1)
            pe.wait_ge(S["ylo_ok"], 4)
            for q in range(2):
                for f in range(4):
                    for t in range(2):
                        c0 = (4 * q + f) * P
                        last = nc.tensor.transpose(mp[q][:, f * NT + t * P:f * NT + (t + 1) * P],
                                                   osb[:, t, c0:c0 + P], ident)
                last.then_inc(S["oT_ps"], 1)

            def reduce_mod(w):
                pe.wait_ge(S["mac_ok"], 16 * w + 16)
                pe.wait_ge(S["mods_ok"], w + 1)
                for t in range(4):
                    last = nc.tensor.matmul(mp[1][:, t:t + 1], wacc[:, t * P:(t + 1) * P], ones[:, 0:1],
                                            start=True, stop=True)
                last.then_inc(S["red_ps"], 1)
            pe.wait_ge(S["olo_ok"], 2)
            with pe.Fori(0, 4) as j:
                it = st.inside(j, 3, (0, 0))
                for i in range(2):
                    pe.wait_ge(S["sg_v"], 2)
                    mm_feature(pe, it, 1 - i, hh, hl, 0, free=(S["mt_ok"], j + 1))
                    reduce_mod(3 * j + i)
                mm_feature(pe, it, 1, yfh, yfl, 0, which=(0, 1), free=(S["gate_ok"], 2 * j + 1))
                mm_feature(pe, it, 0, oh, ol, 0, which=(2, 3), free=(S["gate_ok"], 2 * j + 2))
                reduce_mod(3 * j + 2)
            st.passed(4, 3, (0, 0))

            pe.wait_ge(S["mt_ok"], 5)

            def merged(s):
                pe.wait_ge(S["mlo_ok"], s + 2)
            with pe.Fori(0, 2) as g:
                it = st.inside(g, 2, (1, 1))
                for b in range(2):
                    mm_feature(pe, it, 1 - b, mh, ml, 1, ready=merged)
                    reduce_mod(12 + 2 * g + b)
            st.passed(2, 2, (1, 1))
            norm_sums(pe, 2, mp[0])
            with pe.Fori(0, MLP_CHUNKS) as c:
                it = st.inside(c, 8, (2, 2))
                for g in range(4):
                    mm_feature(pe, it, g % 2, hh, hl, 0, ready=h_ready(pe, 2),
                               free=(S["rsq_ok"], 4 * c + g - 1) if g >= 2 else None)
                for g in range(4):
                    mm_feature(pe, it, g % 2, mh, ml, 1, free=(S["rsq_ok"], 4 * c + g + 3) if g < 2 else None,
                               ready=(lambda s: pe.wait_ge(S["hid_ok"], 4 * c + s + 1)) if g == 0 else None)
            st.passed(MLP_CHUNKS, 8, (2, 2))
            norm_sums(pe, 3, mp[0])
            pe.wait_ge(S["rt_ok"], 4)
            norm_sums(pe, 4, mp[0])
            with pe.Fori(0, 4) as g:
                it = st.inside(g, 2, (1, 1))
                for b in range(2):
                    mm_feature(pe, it, b, hh, hl, 1, ready=h_ready(pe, 3))
            st.passed(4, 2, (1, 1))
            mm_feature(pe, st, 0, hh, hl, 1, ntile=2)
            pe.wait_ge(S["tap_ok"], (KCONV + 1) * TB + 1)
            for t in range(TB):
                last = nc.tensor.matmul(mp[1][:, 0:NT], ones[:, :], uT[:, 24 + t, :], start=t == 0,
                                        stop=t == TB - 1)
            last.then_inc(S["ln_ps"], 1)
            pe.wait_ge(S["pooled_ok"], 1)
            pe.wait_ge(S["pw_in"], 16)
            pe.wait_ge(S["rt_ok"], 5)
            pw = wacc[:, :].rearrange("p (g d) -> p g d", g=TC)
            for t in range(TC):
                last = nc.tensor.matmul(mp[0][:, t * NT:(t + 1) * NT], pw[:, t, :], uT[:, 30 + t, :],
                                        start=True, stop=True)
            last.then_inc(S["pool_ps"], 1)
            pe.wait_ge(S["ln_sq"], 1)
            for t in range(TB):
                last = nc.tensor.matmul(mp[1][:, GC:GC + NT], ones[:, :],
                                        tmp[:, t // 4, (t % 4) * NT:(t % 4 + 1) * NT], start=t == 0,
                                        stop=t == TB - 1)
            last.then_inc(S["ln_ps"], 1)
            pe.wait_ge(S["mxl_ok"], 3)
            with pe.Fori(0, 2) as g:
                it = st.inside(g, 2, (1, 1))
                for b in range(2):
                    mm_feature(pe, it, 1 - b, mh, ml, 1)
            st.passed(2, 2, (1, 1))
            norm_sums(pe, 5, mp[0])
            pe.wait_ge(S["rt_ok"], 6)
            norm_sums(pe, 6, mp[0])

            def ffn(it, c, pairs, slots):
                for p in range(pairs):
                    for v in range(2):
                        mm_feature(pe, it, v, hh, hl, 0, ready=h_ready(pe, 4),
                                   free=(S["cd_ok"], 2 * (4 * c + p) - 1 + v) if p else None)
                for g in range(4):
                    mm_feature(pe, it, g % 2, mh, ml, 1, slots=slots,
                               free=(S["cd_ok"], 2 * (4 * c + pairs) - 1 + g) if g < 2 else None,
                               ready=(lambda s: pe.wait_ge(S["fid_ok"], 4 * c + s + 1)) if g == 0 else None)
            with pe.Fori(0, 2) as c:
                ffn(st.inside(c, 12, (2, 2)), c, 4, 4)
            st.passed(2, 12, (2, 2))
            ffn(st, 2, 3, 3)
            norm_sums(pe, 7, mp[0])
            for q in range(4):
                pe.wait_ge(S["vt_ok"], 8 + q + 1)
                if q >= 2:
                    pe.wait_ge(S["out_sb"], q - 1)
                elif q == 0:
                    pe.wait_ge(S["rt_ok"], 8)
                for t in range(2):
                    for f in range(4):
                        last = nc.tensor.transpose(mp[q % 2][:, t * GC + f * P:t * GC + (f + 1) * P],
                                                   xT2[:, 4 * q + f, t * P:(t + 1) * P], ident)
                last.then_inc(S["out_ps"], 1)


def constants():
    import numpy as np
    t = np.arange(P)
    same = (t[:, None] // CHUNK) == (t[None, :] // CHUNK)
    s, q = t[:, None], t[None, :]
    tau = np.float32(1 / 16)
    con = np.zeros((P, NCON), np.float32)
    con[:, 0:P] = np.eye(P)
    con2 = np.zeros((P, 4 * P + 2), np.float32)
    for n, m in enumerate((s <= q, s >= q, s > q, s < q)):
        con2[:, n * P:(1 + n) * P] = (m & same) * tau
    con2[:, 4 * P:4 * P + 2] = (t[:, None] // CHUNK == np.arange(2)) * tau
    for g in range(4):
        w = 2 << g
        con[:, P + 16 * g:P + 16 * (g + 1)] = w / np.minimum(np.arange(16) + 1.0, w)
    n = np.arange(NT, dtype=np.float64)
    a = 2 * np.pi * ((n[:, None] * n[None, :]) % NT) / NT
    dft = (np.concatenate([np.cos(a), np.sin(a)], 1) / 16).astype(np.float32)
    quarter = D // 4
    omega = np.float32(1) / (np.float32(10000.0) ** (np.arange(quarter, dtype=np.float32) / np.float32(quarter)))
    row = np.repeat(np.arange(NT // 64, dtype=np.float32), 64)
    col = np.tile(np.arange(64, dtype=np.float32), NT // 64)
    er, ec = row[:, None] * omega, col[:, None] * omega
    pos = np.concatenate([np.sin(er), np.cos(er), np.sin(ec), np.cos(ec)], -1).astype(np.float32)
    pos = np.ascontiguousarray(pos.T.reshape(KT, P, NT).transpose(1, 0, 2)).reshape(P, KT * NT)
    return {"con": con, "con2": con2, "dft": dft, "posT": pos}


WEIGHTS = ["w_mod", "w_in", "w_lr_f", "w_lr_b", "w_fourier_out", "w_gla_out", "w_out", "w_mlp_in",
           "w_mlp_out", "w_in_2", "w_out_2", "w_up_2", "w_down_2"]


def kernel(**inputs):
    import numpy as np
    import concourse.bacc as bacc
    from concourse.bass_utils import run_bass_kernel_spmd as run

    x = {k: np.ascontiguousarray(v) for k, v in inputs.items()}
    arrays = dict(constants())
    arrays["x"], arrays["ctx"] = x["x"].reshape(NT, D), x["ctx"].reshape(NT, D)
    for name in WEIGHTS:
        arrays[name] = x[name].reshape(x[name].shape[1:])
    arrays["pool_w_2"] = x["pool_w_2"].reshape(TC * P, P)
    for name in ("b_lr_f", "b_lr_b"):
        arrays[name] = x[name].reshape(1, KEYW)
    for name, n in PROWS:
        arrays[name] = x[name].reshape(n, P)
    nc = bacc.Bacc("TRN2", target_bir_lowering=False, num_devices=1)
    ins = {k: nc.dram_tensor(f"in_{k}", a.shape, mybir.dt.from_np(a.dtype), kind="ExternalInput").ap()
           for k, a in arrays.items()}
    out = nc.dram_tensor("out", (NT, D), mybir.dt.float32, kind="ExternalOutput").ap()
    build(nc, ins, out)
    r = run(nc, [{f"in_{k}": a for k, a in arrays.items()}], core_ids=[0])
    return r.results[0]["out"].reshape(1, NT, D)
```

```python
import concourse.bass as bass
from concourse import mybir
from contextlib import ExitStack

P = 128
D = 2048
NT = 256
KT = D // P
GC = 512
NSLOT = 4
MODS = 6
HEADS, DK, DV = 4, 128, 256
KEYW, VALW, RANK = HEADS * DK, HEADS * DV, 16
CHUNK = 64
FGROUPS, FDIM = 4, 256
C_Q, C_K, C_V = 0, KEYW, 2 * KEYW
C_GOUT = 2 * KEYW + VALW
C_LR = C_GOUT + VALW
C_U = C_LR + 2 * RANK
C_GFFT = C_U + FGROUPS * FDIM
C_GGLA = C_GFFT + D
EPS = 1e-6
LN_EPS = 1e-5
MLP_CHUNKS = 4 * D // 2048
WA, WB, WC = 768, 768, 512
TA, TB, TC = WA // P, WB // P, WC // P
C2_B, C2_C = 3 * WA, 3 * WA + 2 * WB
UT = (C2_C + WC) // P
KCONV = 31
FF2 = 5632
FT = FF2 // P
PROWS = [("c", KT), ("c_ctx", KT), ("b_mod", MODS * KT), ("norm1_g", KT), ("norm2_g", KT),
         ("final_norm_g", KT), ("norm_mix_pre_2", KT), ("norm_mix_post_2", KT), ("norm_ffn_pre_2", KT),
         ("norm_ffn_post_2", KT), ("gla_norm_g", DV // P), ("conv_a_w_2", 3 * TA),
         ("conv_b_w_2", KCONV * TB), ("conv_b_bias_2", TB), ("ln_b_gain_2", TB), ("ln_b_bias_2", TB),
         ("pool_scale_2", TC), ("conv_ffn_w_2", 3 * 2 * FT), ("conv_ffn_bias_2", 2 * FT)]
COL, _n = {}, 0
for _name, _rows in PROWS:
    COL[_name] = _n
    _n += _rows
NPARAM = _n
NPB = -(-NPARAM // P)
NPDMA = sum((COL[n] + r - 1) // P - COL[n] // P + 1 for n, r in PROWS)
NCON = P + 4 * 16 + 2


class Turns:

    def __init__(self, u=(0, 0, 0, 0), f=(0, 0)):
        self.u, self.f = list(u), list(f)

    def inside(self, i, uses, frees):
        return Turns([a + i * uses for a in self.u], [a + i * b for a, b in zip(self.f, frees)])

    def passed(self, n, uses, frees):
        self.u = [a + n * uses for a in self.u]
        self.f = [a + n * b for a, b in zip(self.f, frees)]


def build(nc, ins, out):
    f32, f32r, u32 = mybir.dt.float32, mybir.dt.float32r, mybir.dt.uint32
    ALU, ACT = mybir.AluOpType, mybir.ActivationFunctionType
    ds = bass.ds

    ctx = ExitStack()
    with ctx:
        def sb(name, shape, dt=f32):
            return ctx.enter_context(nc.sbuf_tensor(name, shape, dt))

        def sem(name):
            return ctx.enter_context(nc.semaphore(name))

        def overlay(hold, nbytes, *tensors):
            made = []
            for group in tensors:
                with ExitStack() as own:
                    made += [own.enter_context(nc.sbuf_tensor(n, s, d)) for n, s, d in group]
            sb(hold, [P, nbytes // 4])
            return made

        raw = sb("raw", [P, NSLOT, 4, GC])
        whi = sb("whi", [P, 4, 2, GC], f32r)
        wlo = sb("wlo", [P, 4, 2, GC], f32r)
        hh = sb("hh", [P, KT, NT], f32r)
        hl = sb("hl", [P, KT, NT], f32r)
        tmp = sb("tmp", [P, 2, 4 * NT])
        mrow = sb("mrow", [4, GC])
        pw = sb("pw", [P, TC, P])
        par = sb("par", [P, NPARAM])
        con = sb("con", [P, NCON])
        ones = sb("ones", [P, P])
        rstd = sb("rstd", [P, 2, NT])
        root = sb("root", [P, NT])
        eps = sb("eps", [P, 2])
        csil = sb("csil", [P, 2, KT])
        cv = sb("cv", [P, KT, 4], f32r)
        mpre = sb("mpre", [P, 2, 2, KT])
        mods = sb("mods", [P, 4 * KT])
        a2 = sb("a2", [P, KT])
        fixed = sb("fixed", [P, 4, 16])
        oss = sb("oss", [P, 2, 2 * HEADS])
        (stage_x, posT, ch, cl, lab, keb, tq, state, dft, mh, ml) = overlay(
            "region_a", 32768,
            [("stage_x", [P, 2, D], f32), ("posT", [P, KT, NT], f32)],
            [("ch", [P, KT, NT], f32r), ("cl", [P, KT, NT], f32r)],
            [("lab", [P, 2, KEYW], f32), ("keb", [P, 2, KEYW], f32), ("tq", [P, 2, KEYW], f32),
             ("state", [P, 2, HEADS, DV], f32), ("dft", [P, 2, 2 * NT], f32)],
            [("mh", [P, KT, NT], f32r), ("ml", [P, KT, NT], f32r)])
        (xT, kiT, qdT, sT, wlr, lrn, lrT, dec, con2, yfh, yfl, xT2) = overlay(
            "region_x", 16384,
            [("xT", [P, KT, NT], f32)],
            [("kiT", [P, HEADS * P], f32), ("qdT", [P, HEADS * P], f32), ("sT", [P, 2, HEADS * P], f32),
             ("wlr", [RANK + 1, 2, KEYW], f32), ("lrn", [P, 4, 2, 32], f32), ("lrT", [RANK + 1, P], f32),
             ("dec", [P, HEADS, 2], f32), ("con2", [P, 4 * P + 2], f32)],
            [("yfh", [P, 8, NT], f32r), ("yfl", [P, 8, NT], f32r)],
            [("xT2", [P, KT, NT], f32)])
        (stage_c, ctxT, csig, qn, kn, vn, un, ckn, cvn, oh, ol, sg, osb, pbuf, uT, cacc, yT, up1, up2, outn) = overlay(
            "region_b", 36864,
            [("stage_c", [P, 2, D], f32), ("ctxT", [P, KT, NT], f32), 
             ("csig", [P, 2, KT], f32)],
            [("qn", [P, 2, KEYW], f32), ("kn", [P, 2, KEYW], f32), ("vn", [P, 2, VALW], f32),
             ("un", [P, 2, 1024], f32), ("ckn", [P, 2, KEYW], f32), ("cvn", [P, 2, VALW], f32)],
            [("oh", [P, 8, NT], f32r), ("ol", [P, 8, NT], f32r), ("sg", [P, 8, NT], f32),
             ("osb", [P, 2, VALW], f32), ("pbuf", [P, 2, 2 * NT], f32)],
            [("uT", [P, UT, NT], f32), ("cacc", [P, 2, NT], f32)],
            [("yT", [P, KT, NT], f32), ("up1", [P, 4, NT], f32), ("up2", [P, 4, NT], f32)],
            [("outn", [P, 2, D], f32)])
        spill = nc.dram_tensor("spill", [P, KT * NT], f32, kind="Internal").ap()

        acc = [ctx.enter_context(nc.psum_tensor(f"acc{i}", [P, 4 * NT], f32)) for i in range(2)]
        mp = [ctx.enter_context(nc.psum_tensor(f"mp{i}", [P, 4 * NT], f32)) for i in range(2)]
        ident = con[:, 0:P]
        fix_w = con[:, P:P + 64].rearrange("p (g t) -> p g t", g=4)
        pair_w = con[0:4, P + 64:P + 66]
        cum_w = [con2[:, d * P:(1 + d) * P] for d in range(2)]
        end_w = [con2[:, (2 + d) * P:(3 + d) * P] for d in range(2)]
        half_w = con2[:, 4 * P:4 * P + 2]
        tiles = lambda ap: ap.rearrange("p (t n) -> p t n", n=NT)
        pcol = lambda name, i=0, n=1: par[:, COL[name] + i:COL[name] + i + n]

        raw_full = [sem(f"raw_full{s}") for s in range(NSLOT)]
        hi_done = [sem(f"hi_done{s}") for s in range(NSLOT)]
        lo_done = [sem(f"lo_done{s}") for s in range(NSLOT)]
        used = [sem(f"used{s}") for s in range(NSLOT)]
        acc_free = [sem(f"acc_free{i}") for i in range(2)]
        names = """par_in con_in x_in ctx_in par_ps par_sb csig_ok csil_ok chi_ok cv_ok xt_ps xt_sb ct_sb
            sq_ok ms_ok rt_ok rs_ok tm_ok t2_ok hi_ok lo_ok mod_a mod_b eps_ok spill_ok gla_in dft_in mrow_ok
            mT_ps nat_v a_self v_self
            lrT_ps lrT_sb z_ps ln_ok la_ok cum_ps kexp_ok qexp_ok ke_ok qk_ok qkT_ps qkT_sb sc_ps sc_sb u_ps
            st_ok o_ok oss_ok ort_ok ons_ok oT_ps ot_ok ohi_ok olo_ok p_ps p_sb y_ps yhi_ok ylo_ok
            sg_a mt_ok mhi_ok mlo_ok x_back sg_v relu_ok rsq_ok hhi_ok hid_ok
            bsig_ok tap_ok a_ok mxh_ok mxl_ok pooled_ok pool_ps pool_sb pw_in ln_d ln_sq ln_ps ln_rt
            ln_z ln_sg vt_ok ct_ok cd_ok gs_ok gm_ok fhi_ok fid_ok gate_ok mrg_ok tap2_ok gu_ok out_ps out_sb stored""".split()
        S = {n: sem(n) for n in names}

        block = ctx.enter_context(nc.Block())

        def load(sp, st, w, row0, col0, width=GC, slots=4, srcs=None):
            for s in range(slots):
                src, r = srcs[s] if srcs else (w, row0 + 512 * s)
                if not (isinstance(st.u[s], int) and st.u[s] == 0):
                    sp.wait_ge(lo_done[s], 2 * st.u[s])
                rows = src[ds(r, 512), ds(col0, width)].rearrange("(k p) n -> p k n", p=P)
                sp.dma_start(raw[:, s, :, 0:width], rows).then_inc(raw_full[s], 16)
                st.u[s] = st.u[s] + 1

        def pieces(slots):
            return [(s, j, (2 * s + j) % 4) for s in slots for j in range(2)]

        def conv_hi(act, st, slots, width=GC, after3=False):
            for s, j, _ in pieces(slots):
                hi_piece(act, st, s, j, width, after3)

        def hi_piece(act, st, s, j, width=GC, after3=False):
            r = (2 * s + j) % 4
            o = (s + 2) % 4
            if j == 0:
                act.wait_ge(raw_full[s], 16 * st.u[s] + 16)
            if not (isinstance(st.u[o], int) and st.u[o] == 0):
                act.wait_ge(used[o], 2 * st.u[o] - 1 + j)
            if after3 and s == 1:
                act.wait_ge(used[s], 2 * st.u[s] - 1 + j)
            nc.scalar.activation(whi[:, r, :, 0:width], raw[:, s, 2 * j:2 * j + 2, 0:width],
                                 ACT.Copy).then_inc(hi_done[s], 1)
            if j == 1:
                st.u[s] = st.u[s] + 1

        def conv_lo(dve, st, slots, width=GC, behind=None):
            for s, j, _ in pieces(slots):
                lo_piece(dve, st, s, j, width)
                if behind:
                    behind()

        def lo_piece(dve, st, s, j, width=GC):
            r = (2 * s + j) % 4
            dve.wait_ge(hi_done[s], 2 * st.u[s] + j + 1)
            nc.vector.tensor_tensor(wlo[:, r, :, 0:width], raw[:, s, 2 * j:2 * j + 2, 0:width],
                                    whi[:, r, :, 0:width].bitcast(f32),
                                    ALU.subtract).then_inc(lo_done[s], 1)
            if j == 1:
                st.u[s] = st.u[s] + 1

        def split_ahead(conv, st, slots=4, nslots=4, width=GC, nwidth=GC, last=False, **kw):
            if slots > 2:
                conv(st, range(2, slots), width, **kw)
            if not last:
                conv(st, range(min(2, nslots)), nwidth, **kw)

        def group_done(eng, st, slots=4):
            eng.wait_ge(used[slots - 1], 2 * st.u[slots - 1])

        def mm_feature(pe, st, i, hi, lo, frees, slots=4, first=0, ntile=4, into=None, ready=None,
                       which=None, free=None):
            which = range(slots) if which is None else which
            if free:
                pe.wait_ge(*free)
            else:
                pe.wait_ge(acc_free[i], st.f[i])
            for n, s in enumerate(which):
                if ready:
                    ready(n)
                for j in range(2):
                    r = (2 * s + j) % 4
                    pe.wait_ge(lo_done[s], 2 * st.u[s] + j + 1)
                    for k in range(2):
                        kt = first + 4 * n + 2 * j + k
                        for t in range(ntile):
                            dst = acc[i][:, t * NT:(t + 1) * NT]
                            cols = slice(t * P, (t + 1) * P)
                            begin = kt == first and t % 2 == 0
                            nc.tensor.matmul(dst, whi[:, r, k, cols], hi[:, kt, :], start=begin, stop=False,
                                             skip_group_check=True)
                            nc.tensor.matmul(dst, whi[:, r, k, cols], lo[:, kt, :], start=False, stop=False,
                                             skip_group_check=True)
                            last = nc.tensor.matmul(dst, wlo[:, r, k, cols], hi[:, kt, :], start=False,
                                                    stop=kt == first + 4 * len(which) - 1,
                                                    skip_group_check=True)
                    last.then_inc(used[s], 1)
                st.u[s] = st.u[s] + 1
            st.f[i] = st.f[i] + frees

        def mod_piece(pe, st, i, s, j):
            r = (2 * s + j) % 4
            if s + j == 0 and not (isinstance(st.f[i], int) and st.f[i] == 0):
                pe.wait_ge(acc_free[i], st.f[i])
            pe.wait_ge(lo_done[s], 2 * st.u[s] + j + 1)
            for k in range(2):
                kt = 4 * s + 2 * j + k
                nc.tensor.matmul(acc[i][0:4, 0:GC], cv[:, kt, :], whi[:, r, k, :], start=kt == 0, stop=False)
                last = nc.tensor.matmul(acc[i][0:4, 0:GC], cv[:, kt, :], wlo[:, r, k, :], start=False,
                                        stop=kt == KT - 1)
            last.then_inc(used[s], 1)
            if j == 1:
                st.u[s] = st.u[s] + 1
                if s == 3:
                    st.f[i] = st.f[i] + 1

        def mod_turn(pe, n, i):
            pe.wait_ge(S["mrow_ok"], n + 1)
            for t in range(4):
                last = nc.tensor.matmul(acc[i][:, GC + 2 * t:GC + 2 * t + 2], mrow[:, t * P:(t + 1) * P], pair_w,
                                        start=True, stop=True)
            last.then_inc(S["mT_ps"], 1)

        def mod_row(dve, st, i):
            group_done(dve, st)
            nc.vector.tensor_copy(mrow[:, :], acc[i][0:4, 0:GC]).then_inc(S["mrow_ok"], 1)

        def mod_out(dve, n, i):
            dve.wait_ge(S["mT_ps"], n + 1)
            col = acc[i][:, GC:GC + 8].rearrange("p (t v) -> p v t", v=2)
            bias = par[:, ds(4 * n + COL["b_mod"], 4)].rearrange("p (a t) -> p a t", a=1)
            if isinstance(n, int) and n >= 8:
                out = mods[:, 4 * (n - 8):4 * (n - 7)].rearrange("p (a t) -> p a t", a=1)
                col = col[:, 0:1, :]
            else:
                out = mpre[:, :, :, :].rearrange("p v a k -> p v (a k)")[:, :, ds(4 * n, 4)]
                bias = bias.to_broadcast([P, 2, 4])
            nc.vector.tensor_tensor(out, col, bias, ALU.add).then_inc(acc_free[i], 1)

        class Ticks:

            def __init__(self):
                self.n = 0

            def step(self):
                n = self.n
                self.n += 1
                return n, n // 8 + 8, (n % 8) // 2, n % 2

        def mod_ticks_pe(pe, st, ticks, count):
            for _ in range(count):
                n, g, s, j = ticks.step()
                mod_piece(pe, st, (g + 1) % 2, s, j)
                if n % 8 == 3 and n > 8:
                    mod_turn(pe, g - 1, g % 2)

        def mod_ticks_act(act, st, ticks, count):
            for _ in range(count):
                _, _, s, j = ticks.step()
                hi_piece(act, st, (s + 2) % 4, j)

        def mod_ticks_dve(dve, st, ticks, count):
            for _ in range(count):
                n, g, s, j = ticks.step()
                if n % 8 == 0 and n:
                    mod_row(dve, st, g % 2)
                if n % 8 == 4 and n > 8:
                    mod_out(dve, g - 1, g % 2)
                lo_piece(dve, st, (s + 2) % 4, j)

        def mm_token(pe, st, i, width, with_ctx, ready=None):
            if st.f[i]:
                pe.wait_ge(acc_free[i], st.f[i])
            outs = [(acc[i], 0, hh, hl, 0, width), (acc[i], GC, hh, hl, P, width)]
            if with_ctx:
                outs += [(mp[i], 0, ch, cl, 0, with_ctx), (mp[i], GC, ch, cl, P, with_ctx)]
            for s in range(4):
                if ready:
                    ready(s)
                for j in range(2):
                    r = (2 * s + j) % 4
                    pe.wait_ge(lo_done[s], 2 * st.u[s] + j + 1)
                    for k in range(2):
                        kt = 4 * s + 2 * j + k
                        for bank, off, hi, lo, t0, w in outs:
                            dst = bank[:, off:off + w]
                            nc.tensor.matmul(dst, hi[:, kt, t0:t0 + P], whi[:, r, k, 0:w], start=kt == 0,
                                             stop=False)
                            nc.tensor.matmul(dst, hi[:, kt, t0:t0 + P], wlo[:, r, k, 0:w], start=False,
                                             stop=False)
                            last = nc.tensor.matmul(dst, lo[:, kt, t0:t0 + P], whi[:, r, k, 0:w],
                                                    start=False, stop=kt == KT - 1)
                    last.then_inc(used[s], 1)
                st.u[s] += 1
            st.f[i] += 2 if with_ctx else 1

        TOKEN = [(C_K, GC, GC), (C_V, GC, GC), (C_V + GC, GC, GC), (C_LR, GC, 2 * RANK), (C_Q, GC, 0),
                 (C_LR + GC, GC, 0), (C_LR + 2 * GC, C_GFFT - C_LR - 2 * GC, 0)]
        NEXT_W = [w for _, w, _ in TOKEN[1:]] + [GC]
        F_TOKEN = [4 + sum(2 if cw else 1 for n, (_, _, cw) in enumerate(TOKEN) if n % 2 == i) for i in range(2)]
        F_MOD = [f + 8 for f in F_TOKEN]
        F_OUT = [f + 2 for f in F_MOD]
        F_MLP = [f + 2 * MLP_CHUNKS for f in F_OUT]
        F_UB = [f + 2 for f in F_MLP]
        F_U = [F_UB[0] + 3, F_UB[1] + 2]
        F_OUT2 = [f + 2 for f in F_U]
        F_FFN = [f + 6 for f in F_OUT2]

        def all_read(eng, counts):
            for i in range(2):
                eng.wait_ge(acc_free[i], counts[i])

        SCANS = [(src, d, t) for src in range(2) for d in range(2) for t in ((0, 1), (1, 0))[d]]

        T_LR, T_Z, T_CUM, T_QK, T_SC, T_STATE, T_FFT, T_ONORM = 2, (3, 3), (2, 3), 2, 2, 2, 2, 4
        assert 4 * (2 * T_LR + sum(T_Z) + sum(T_CUM) + T_QK + T_SC + 4 * T_STATE + 2 * T_FFT) + T_ONORM == 128

        def norm_squares(act, k, src):
            for q in range(4):
                n = 4 * k + q
                if n >= 2:
                    act.wait_ge(S["ms_ok"], n - 1)
                nc.scalar.activation(tiles(tmp[:, q % 2, :]), src[:, 4 * q:4 * q + 4, :], ACT.Square)\
                    .then_inc(S["sq_ok"], 1)

        def norm_sums(pe, k, bank):
            for q in range(4):
                pe.wait_ge(S["sq_ok"], 4 * k + q + 1)
                for t in range(4):
                    last = nc.tensor.matmul(bank[:, 0:NT], ones[:, :], tmp[:, q % 2, t * NT:(t + 1) * NT],
                                            start=q + t == 0, stop=q + t == 6)
                last.then_inc(S["ms_ok"], 1)

        def norm_root(act, k, bank, n=D, e=0):
            act.wait_ge(S["ms_ok"], 4 * k + 4)
            if k:
                act.wait_ge(S["rs_ok"], k)
            nc.scalar.activation(root[:, :], bank[:, 0:NT], ACT.Sqrt, bias=eps[:, e:e + 1],
                                 scale=1.0 / n).then_inc(S["rt_ok"], 1)

        def norm_rstd(dve, k):
            dve.wait_ge(S["rt_ok"], k + 1)
            nc.vector.reciprocal(rstd[:, k % 2, :], root[:, :]).then_inc(S["rs_ok"], 1)

        def rbc(k, n=4):
            return rstd[:, k % 2:k % 2 + 1, :].to_broadcast([P, n, NT])

        def apply_dve(dve, n0, norms, jobs):
            def times(i):
                n = n0 + i
                src, k, hi, lo, q = jobs[i]
                if i == 0:
                    dve.wait_ge(S["rs_ok"], norms)
                    dve.wait_ge(S["ms_ok"], 4 * norms)
                if n >= 2:
                    dve.wait_ge(S["lo_ok"], n - 1)
                nc.vector.tensor_tensor(tiles(tmp[:, n % 2, :]), src[:, 4 * q:4 * q + 4, :], rbc(k),
                                        ALU.mult).then_inc(S["tm_ok"], 1)

            def rest(i):
                n = n0 + i
                src, k, hi, lo, q = jobs[i]
                dve.wait_ge(S["hi_ok"], n + 1)
                nc.vector.tensor_tensor(lo[:, 4 * q:4 * q + 4, :], tiles(tmp[:, n % 2, :]),
                                        hi[:, 4 * q:4 * q + 4, :].bitcast(f32),
                                        ALU.subtract).then_inc(S["lo_ok"], 1)
            times(0)
            for i in range(len(jobs)):
                if i + 1 < len(jobs):
                    times(i + 1)
                rest(i)

        def apply_act(act, n0, jobs):
            for i, (hi, scale, shift, q) in enumerate(jobs):
                n = n0 + i
                act.wait_ge(S["tm_ok"], n + 1)
                for t in range(4):
                    kt = 4 * q + t
                    part = tmp[:, n % 2, t * NT:(t + 1) * NT]
                    last = nc.scalar.activation(part, part, ACT.Identity,
                                                bias=shift(kt) if shift else 0.0, scale=scale(kt))
                last.then_inc(S["t2_ok"], 1)
                act.wait_ge(S["t2_ok"], n + 1)
                nc.scalar.activation(hi[:, 4 * q:4 * q + 4, :], tiles(tmp[:, n % 2, :]), ACT.Copy)\
                    .then_inc(S["hi_ok"], 1)

        def h_ready(pe, n0, per=1):
            def wait(s):
                pe.wait_ge(S["lo_ok"], n0 + per * (s + 1))
            return wait

        @block.sync
        def _(sp):
            rows = tmp[:, 0, 0:NPB * P].rearrange("p (b n) -> p b n", b=NPB)
            for name, n in PROWS:
                done = 0
                while done < n:
                    r = COL[name] + done
                    m = min(n - done, P - r % P)
                    sp.dma_start(rows[r % P:r % P + m, r // P, :], ins[name][done:done + m, :])\
                        .then_inc(S["par_in"], 16)
                    done += m
            st = Turns()
            load(sp, st, ins["w_mod"], 0, 0)
            with sp.Fori(0, 7) as g:
                load(sp, st.inside(g, 1, (0, 0)), ins["w_mod"], 0, GC * g + GC)
            st.passed(7, 1, (0, 0))
            for c0, width, _ in TOKEN:
                load(sp, st, ins["w_in"], 0, c0, width)
            with sp.Fori(0, 16) as g:
                load(sp, st.inside(g, 1, (0, 0)), ins["w_mod"], 0, 2 * D + GC * g)
            st.passed(16, 1, (0, 0))
            for g in range(2):
                load(sp, st, ins["w_in"], 0, C_GOUT + GC * g)
            with sp.Fori(1, 5) as j:
                it = st.inside(j - 1, 3, (0, 0))
                load(sp, it, ins["w_in"], 0, C_GFFT - GC + GC * j)
                load(sp, it, ins["w_in"], 0, C_GGLA - GC + GC * j)
                load(sp, it, None, 0, GC * j - GC, srcs=[(ins["w_fourier_out"], 0), (ins["w_fourier_out"], 512),
                                                    (ins["w_gla_out"], 0), (ins["w_gla_out"], 512)])
            st.passed(4, 3, (0, 0))
            with sp.Fori(0, 4) as g:
                load(sp, st.inside(g, 1, (0, 0)), ins["w_out"], 0, GC * g)
            st.passed(4, 1, (0, 0))
            with sp.Fori(0, MLP_CHUNKS) as c:
                it = st.inside(c, 8, (0, 0))
                for g in range(4):
                    load(sp, it, ins["w_mlp_in"], 0, 2048 * c + GC * g)
                for g in range(4):
                    load(sp, it, ins["w_mlp_out"], 2048 * c, GC * g)
            st.passed(MLP_CHUNKS, 8, (0, 0))
            with sp.Fori(0, 4) as g:
                load(sp, st.inside(g, 1, (0, 0)), ins["w_in_2"], 0, C2_B + GC * g)
            st.passed(4, 1, (0, 0))
            with sp.Fori(0, 4) as g:
                load(sp, st.inside(g, 1, (0, 0)), ins["w_in_2"], 0, GC * g)
            st.passed(4, 1, (0, 0))
            load(sp, st, ins["w_in_2"], 0, 4 * GC, C2_B - 4 * GC)
            with sp.Fori(0, 4) as g:
                load(sp, st.inside(g, 1, (0, 0)), ins["w_out_2"], 0, GC * g)
            st.passed(4, 1, (0, 0))

            def ffn(it, c, pairs, slots):
                for p in range(pairs):
                    load(sp, it, ins["w_up_2"], 0, 2048 * c + GC * p)
                    load(sp, it, ins["w_up_2"], 0, FF2 + 2048 * c + GC * p)
                for g in range(4):
                    load(sp, it, ins["w_down_2"], 2048 * c, GC * g, slots=slots)
            with sp.Fori(0, 2) as c:
                ffn(st.inside(c, 12, (0, 0)), c, 4, 4)
            st.passed(2, 12, (0, 0))
            ffn(st, 2, 3, 3)
            sp.wait_ge(S["out_sb"], 4)
            sp.dma_start(out.rearrange("(t p) d -> p t d", p=P), outn[:, :, :]).then_inc(S["stored"], 16)
            sp.wait_ge(S["stored"], 16)

        @block.gpsimd
        def _(pool):
            pool.wait_ge(S["xt_sb"], 4)
            pool.dma_start(spill, xT[:, :, :].rearrange("p t n -> p (t n)")).then_inc(S["spill_ok"], 16)
            pool.wait_ge(S["spill_ok"], 16)
            pool.wait_ge(S["lo_ok"], 7)
            for d, (w, b) in enumerate((("w_lr_f", "b_lr_f"), ("w_lr_b", "b_lr_b"))):
                pool.dma_start(wlr[0:RANK, d, :], ins[w]).then_inc(S["gla_in"], 16)
                pool.dma_start(wlr[RANK:RANK + 1, d, :], ins[b]).then_inc(S["gla_in"], 16)
            pool.dma_start(con2[:, :], ins["con2"]).then_inc(S["gla_in"], 16)
            pool.wait_ge(S["nat_v"], 4)
            pool.dma_start(dft[:, :, :], ins["dft"].rearrange("(t p) n -> p t n", p=P))\
                .then_inc(S["dft_in"], 16)

            pool.wait_ge(S["mlo_ok"], 5)
            pool.dma_start(xT2[:, :, :].rearrange("p t n -> p (t n)"), spill).then_inc(S["x_back"], 16)
            pool.dma_start(pw[:, :, :], ins["pool_w_2"].rearrange("(g p) d -> p g d", p=P)).then_inc(S["pw_in"], 16)

        @block.scalar
        def _(act):
            act.dma_start(con[:, :], ins["con"]).then_inc(S["con_in"], 16)
            act.dma_start(stage_x[:, :, :], ins["x"].rearrange("(t p) d -> p t d", p=P)).then_inc(S["x_in"], 16)
            act.dma_start(posT[:, :, :].rearrange("p t n -> p (t n)"), ins["posT"]).then_inc(S["x_in"], 16)
            act.dma_start(stage_c[:, :, :], ins["ctx"].rearrange("(t p) d -> p t d", p=P))\
                .then_inc(S["ctx_in"], 16)
            st = Turns()

            def own(n):
                act.wait_ge(S["a_self"], n)

            conv_hi(act, st, (0, 1))
            act.wait_ge(S["par_sb"], 1)
            nc.scalar.activation(csig[:, :, :], pcol("c", 0, 2 * KT).rearrange("p (v k) -> p v k", v=2),
                                 ACT.Sigmoid).then_inc(S["csig_ok"], 1)
            act.wait_ge(S["csil_ok"], 1)
            nc.scalar.activation(cv[:, :, 0:2], csil[:, :, :].rearrange("p v k -> p k v"), ACT.Copy)\
                .then_inc(S["chi_ok"], 1)
            for g in range(2):
                split_ahead(lambda *a, **k: conv_hi(act, *a, **k), st)
            for q in range(4):
                act.wait_ge(S["xt_ps"], 5 + q)
                nc.scalar.activation(ctxT[:, 4 * q:4 * q + 4, :], tiles(mp[q % 2][:, :]), ACT.Copy)\
                    .then_inc(S["ct_sb"], 1)
            act.wait_ge(S["xt_sb"], 4)
            act.wait_ge(S["eps_ok"], 3)
            norm_squares(act, 0, xT)
            act.wait_ge(S["ct_sb"], 4)
            norm_squares(act, 1, ctxT)
            norm_root(act, 0, mp[0])
            norm_root(act, 1, mp[1])
            C = lambda *a, **k: conv_hi(act, *a, **k)
            with act.Fori(0, 3) as g:
                it = st.inside(g, 2, (0, 0))
                for b in range(2):
                    split_ahead(C, it)
            st.passed(3, 2, (0, 0))
            act.wait_ge(S["mod_a"], 1)
            first = [(hi, lambda kt, v=v: mpre[:, v, 1, kt:kt + 1], lambda kt, v=v: mpre[:, v, 0, kt:kt + 1])
                     for v, hi in enumerate((hh, ch))]
            apply_act(act, 0, [(*job, q) for q in range(4) for job in first])
            for n, (c0, width, cw) in enumerate(TOKEN):
                split_ahead(C, st, width=width, nwidth=NEXT_W[n])
                if cw:
                    group_done(act, st)
                    src = mp[n % 2][:, :].rearrange("p (t n) -> p t n", t=2)
                    if c0 == C_LR:
                        act.wait_ge(S["spill_ok"], 16)
                        dst = lrn[:, 2:4, :, 0:RANK]
                        src = mp[n % 2][:, :].rearrange("p (t n) -> p t n", t=2)[:, :, 0:cw]\
                            .rearrange("p t (d r) -> p t d r", d=2)
                        for t in range(2):
                            last = nc.scalar.activation(dst[:, t], src[:, t], ACT.Copy)
                    else:
                        dst = ckn[:, :, :] if c0 == C_K else cvn[:, :, c0 - C_V:c0 - C_V + GC]
                        last = nc.scalar.activation(dst, src, ACT.Copy)
                    last.then_inc(acc_free[n % 2], 1)
            ticks = Ticks()
            tick = lambda count: mod_ticks_act(act, st, ticks, count)
            a_n = 0
            sts = 0
            for m, (src, d, t) in enumerate(SCANS):
                l = m - 4
                tick(T_LR)
                act.wait_ge(S["z_ps"], m + 1)
                if m:
                    act.wait_ge(S["ke_ok"], m)
                nc.scalar.activation(tq[:, 0, :], mp[0][:, GC:2 * GC], ACT.Abs).then_inc(S["a_self"], 1)
                own(a_n + 1)
                nc.scalar.activation(tq[:, 0, :], tq[:, 0, :], ACT.Exp, scale=-1.0).then_inc(S["a_self"], 1)
                own(a_n + 2)
                a_n += 2
                nc.scalar.activation(tq[:, 0, :], tq[:, 0, :], ACT.Ln, bias=1.0).then_inc(S["ln_ok"], 1)
                tick(T_Z[src])
                act.wait_ge(S["cum_ps"], m + 1)
                if sts:
                    act.wait_ge(S["st_ok"], sts)
                nc.scalar.activation(dec[:, :, :].rearrange("p h c -> p (h c)"), mp[0][:, 0:2 * HEADS],
                                     ACT.Exp)
                nc.scalar.activation(tq[:, 1, :], mp[1][:, 0:GC], ACT.Exp).then_inc(S["kexp_ok"], 1)
                if src:
                    nc.scalar.activation(tmp[:, 0, 0:GC], mp[1][:, GC:2 * GC], ACT.Exp)
                    nc.scalar.activation(tmp[:, 0, GC:2 * GC], mp[1][:, GC:2 * GC], ACT.Exp, scale=-1.0)\
                        .then_inc(S["qexp_ok"], 1)
                tick(T_CUM[src])
                if src:
                    act.wait_ge(S["qkT_ps"], l + 1)
                    nc.scalar.activation(kiT[:, :], mp[0][:, GC:2 * GC], ACT.Copy).then_inc(S["qkT_sb"], 1)
                    tick(T_QK)
                    tick(T_SC)
                tick(T_STATE)
                tick(T_STATE)
                sts += 1 if src and t == (1, 0)[d] else 2
            tick(T_ONORM)
            act.wait_ge(S["o_ok"], 4)
            for t in range(2):
                for h in range(HEADS):
                    n = t * HEADS + h
                    last = nc.scalar.activation(tmp[:, t, h * DV:(h + 1) * DV], osb[:, t, h * DV:(h + 1) * DV],
                                                ACT.Square, accum_out=oss[:, 0, n:n + 1])
            last.then_inc(S["oss_ok"], 1)
            act.wait_ge(S["oss_ok"], 1)
            nc.scalar.activation(oss[:, 1, :], oss[:, 0, :], ACT.Sqrt, bias=eps[:, 0:1], scale=1.0 / DV)\
                .then_inc(S["ort_ok"], 1)
            for g in range(FGROUPS):
                act.wait_ge(S["p_ps"], g + 1)
                if g:
                    act.wait_ge(S["y_ps"], g)
                pv = mp[0][:, :].rearrange("p (t n) -> p t n", t=2)
                nc.scalar.activation(pbuf[:, :, 0:NT], pv[:, :, 0:NT], ACT.Copy)
                nc.scalar.activation(pbuf[:, :, NT:2 * NT], pv[:, :, NT:2 * NT], ACT.Copy, scale=-1.0)\
                    .then_inc(S["p_sb"], 1)
                tick(T_FFT)
                act.wait_ge(S["y_ps"], g + 1)
                nc.scalar.activation(yfh[:, 2 * g:2 * g + 2, :], tiles(mp[1][:, 0:2 * NT]), ACT.Copy)\
                    .then_inc(S["yhi_ok"], 1)
                tick(T_FFT)
            for g in range(2):
                split_ahead(C, st)
                group_done(act, st)
                nc.scalar.activation(sg[:, 4 * g:4 * g + 4, :], tiles(acc[(7 + g) % 2][:, :]), ACT.Sigmoid)\
                    .then_inc(S["sg_a"], 1)
            for q in range(2):
                act.wait_ge(S["ot_ok"], q + 1)
                nc.scalar.activation(oh[:, 4 * q:4 * q + 4, :], tiles(tmp[:, q, :]), ACT.Copy)\
                    .then_inc(S["ohi_ok"], 1)
            act.wait_ge(S["olo_ok"], 2)
            with act.Fori(0, 4) as j:
                it = st.inside(j, 3, (0, 0))
                act.wait_ge(S["mlo_ok"], j + 1)
                for i in range(2):
                    split_ahead(C, it)
                    group_done(act, it)
                    nc.scalar.activation(tmp[:, i, :], acc[1 - i][:, :], ACT.Sigmoid)\
                        .then_inc(S["gate_ok"], 1)
                split_ahead(C, it)
                act.wait_ge(S["mt_ok"], j + 1)
                nc.scalar.activation(mh[:, ds(4 * j, 4), :], tiles(tmp[:, 0, :]), ACT.Copy)\
                    .then_inc(S["mhi_ok"], 1)
            st.passed(4, 3, (0, 0))
            with act.Fori(0, 4) as g:
                split_ahead(C, st.inside(g, 1, (0, 0)))
            st.passed(4, 1, (0, 0))
            all_read(act, F_OUT)
            norm_squares(act, 2, xT2)
            norm_root(act, 2, mp[0])
            act.wait_ge(S["mod_b"], 1)
            apply_act(act, 8, [(hh, lambda kt: a2[:, kt:kt + 1], lambda kt: mods[:, KT + kt:KT + kt + 1], q)
                               for q in range(4)])
            act.wait_ge(S["lo_ok"], 12)
            with act.Fori(0, MLP_CHUNKS) as c:
                it = st.inside(c, 8, (0, 0))
                for g in range(4):
                    n = 4 * c + g
                    split_ahead(C, it)
                    group_done(act, it)
                    nc.scalar.activation(tmp[:, 0, :], acc[g % 2][:, :], ACT.Relu).then_inc(S["relu_ok"], 1)
                    act.wait_ge(S["rsq_ok"], n + 1)
                    nc.scalar.activation(mh[:, 4 * g:4 * g + 4, :], tiles(tmp[:, 1, :]), ACT.Copy)\
                        .then_inc(S["hhi_ok"], 1)
                for g in range(4):
                    split_ahead(C, it)
            st.passed(MLP_CHUNKS, 8, (0, 0))
            all_read(act, F_MLP)
            norm_squares(act, 3, xT2)
            norm_root(act, 3, mp[0])
            act.wait_ge(S["vt_ok"], 4)
            norm_squares(act, 4, xT2)
            norm_root(act, 4, mp[0])
            apply_act(act, 12, [(hh, lambda kt: pcol("norm_mix_pre_2", kt), None, q) for q in range(4)])
            with act.Fori(0, 2) as g:
                it = st.inside(g, 2, (0, 0))
                for b in range(2):
                    split_ahead(C, it)
            st.passed(2, 2, (0, 0))
            all_read(act, F_UB)
            nc.scalar.activation(uT[:, 24:30, :], uT[:, 24:30, :], ACT.Sigmoid).then_inc(S["bsig_ok"], 1)
            with act.Fori(0, 2) as g:
                it = st.inside(g, 2, (0, 0))
                for b in range(2):
                    split_ahead(C, it)
            st.passed(2, 2, (0, 0))
            split_ahead(C, st, width=C2_B - 4 * GC)
            tf = tmp[:, :, :].rearrange("p a n -> p (a n)")
            act.wait_ge(S["a_ok"], 1)
            nc.scalar.activation(mh[:, 0:TA, :], uT[:, 12:12 + TA, :], ACT.Copy).then_inc(S["mxh_ok"], 1)
            act.wait_ge(S["pool_ps"], 1)
            for t in range(TC):
                last = nc.scalar.activation(uT[:, 30 + t, :], mp[0][:, t * NT:(t + 1) * NT], ACT.Copy,
                                            scale=pcol("pool_scale_2", t))
            last.then_inc(S["pool_sb"], 1)
            act.wait_ge(S["pool_sb"], 1)
            nc.scalar.activation(mh[:, TA + TB:KT, :], uT[:, 30:34, :], ACT.Copy).then_inc(S["mxh_ok"], 1)
            act.wait_ge(S["ln_d"], 1)
            nc.scalar.activation(tf[:, 0:WB * 2], uT[:, 24:30, :].rearrange("p t n -> p (t n)"), ACT.Square)\
                .then_inc(S["ln_sq"], 1)
            act.wait_ge(S["ln_ps"], 2)
            nc.scalar.activation(root[:, :], mp[1][:, GC:GC + NT], ACT.Sqrt, bias=eps[:, 1:2], scale=1.0 / WB)\
                .then_inc(S["ln_rt"], 1)
            act.wait_ge(S["ln_d"], 2)
            for t in range(TB):
                last = nc.scalar.activation(uT[:, 24 + t, :], uT[:, 24 + t, :], ACT.Identity,
                                            bias=pcol("ln_b_bias_2", t), scale=pcol("ln_b_gain_2", t))
            last.then_inc(S["ln_z"], 1)
            act.wait_ge(S["ln_z"], 1)
            nc.scalar.activation(tf[:, 0:WB * 2], uT[:, 24:30, :].rearrange("p t n -> p (t n)"), ACT.Sigmoid)\
                .then_inc(S["ln_sg"], 1)
            act.wait_ge(S["ln_d"], 3)
            nc.scalar.activation(mh[:, TA:TA + TB, :], uT[:, 24:30, :], ACT.Copy).then_inc(S["mxh_ok"], 1)
            with act.Fori(0, 4) as g:
                split_ahead(C, st.inside(g, 1, (0, 0)))
            st.passed(4, 1, (0, 0))
            all_read(act, F_OUT2)
            norm_squares(act, 5, yT)
            norm_root(act, 5, mp[0])
            act.wait_ge(S["vt_ok"], 8)
            norm_squares(act, 6, xT2)
            norm_root(act, 6, mp[0])
            apply_act(act, 16, [(hh, lambda kt: pcol("norm_ffn_pre_2", kt), None, q) for q in range(4)])
            act.wait_ge(S["lo_ok"], 20)

            def ffn_pair(it, c, p, n, **kw):
                for v in range(2):
                    split_ahead(C, it, **(kw if v else {}))
                    group_done(act, it)
                    up = (up1, up2)[v]
                    for t in range(4):
                        col = 16 * c + 4 * p + t + FT * v
                        last = nc.scalar.activation(
                            up[:, t, :], acc[v][:, t * NT:(t + 1) * NT], ACT.Identity,
                            bias=par[:, ds(COL["conv_ffn_bias_2"] + col, 1)],
                            scale=par[:, ds(COL["conv_ffn_w_2"] + 4 * FT + col, 1)])
                    last.then_inc(S["ct_ok"], 1)
                    act.wait_ge(S["cd_ok"], 2 * n + v + 1)
                    if v == 0:
                        nc.scalar.activation(tiles(tmp[:, 0, :]), up1[:, :, :], ACT.Sigmoid)\
                            .then_inc(S["gs_ok"], 1)
                    else:
                        act.wait_ge(S["gm_ok"], n + 1)
                        nc.scalar.activation(mh[:, 4 * p:4 * p + 4, :], tiles(tmp[:, 1, :]), ACT.Copy)\
                            .then_inc(S["fhi_ok"], 1)
            with act.Fori(0, 2) as c:
                it = st.inside(c, 12, (0, 0))
                for p in range(4):
                    ffn_pair(it, c, p, 4 * c + p)
                for g in range(4):
                    split_ahead(C, it)
            st.passed(2, 12, (0, 0))
            for p in range(3):
                ffn_pair(st, 2, p, 8 + p)
            for g in range(4):
                split_ahead(C, st, slots=3, last=g == 3, after3=True)
            all_read(act, F_FFN)
            norm_squares(act, 7, yT)
            norm_root(act, 7, mp[0])

        @block.vector
        def _(dve):
            st = Turns()
            seen = [0]

            def own(ins):
                ins.then_inc(S["v_self"], 1)
                seen[0] += 1
                dve.wait_ge(S["v_self"], seen[0])

            for name, n in (("mrg_ok", 2), ("mlo_ok", 1), ("tap_ok", 1)):
                dve.sem_inc(S[name], n)
            nc.vector.memset(ones[:, :], 1.0).then_inc(S["eps_ok"], 1)
            nc.vector.memset(eps[:, 0:1], EPS).then_inc(S["eps_ok"], 1)
            nc.vector.memset(eps[:, 1:2], LN_EPS).then_inc(S["eps_ok"], 1)
            conv_lo(dve, st, (0, 1))
            dve.wait_ge(S["par_ps"], 1)
            nc.vector.tensor_copy(par[:, :], mp[1][:, 0:NPARAM]).then_inc(S["par_sb"], 1)
            dve.wait_ge(S["par_sb"], 1)
            dve.wait_ge(S["csig_ok"], 1)
            nc.vector.tensor_tensor(csil[:, :, :], pcol("c", 0, 2 * KT).rearrange("p (v k) -> p v k", v=2),
                                    csig[:, :, :], ALU.mult).then_inc(S["csil_ok"], 1)
            dve.wait_ge(S["csil_ok"], 1)
            dve.wait_ge(S["chi_ok"], 1)
            nc.vector.tensor_tensor(cv[:, :, 2:4], csil[:, :, :].rearrange("p v k -> p k v"),
                                    cv[:, :, 0:2].bitcast(f32), ALU.subtract).then_inc(S["cv_ok"], 1)
            C = lambda *a, **k: conv_lo(dve, *a, **k)

            def mod_evac(it, n, i):
                C(it, (2, 3))
                if not isinstance(n, int) or n:
                    mod_out(dve, n - 1, 1 - i)
                C(it, (0, 1))
                mod_row(dve, it, i)
            for g in range(2):
                mod_evac(st, g, g)
            dve.wait_ge(S["x_in"], 32)
            for q in range(4):
                dve.wait_ge(S["xt_ps"], q + 1)
                nc.vector.tensor_tensor(xT[:, 4 * q:4 * q + 4, :], tiles(mp[q % 2][:, :]),
                                        posT[:, 4 * q:4 * q + 4, :], ALU.add).then_inc(S["xt_sb"], 1)
            norm_rstd(dve, 0)
            norm_rstd(dve, 1)
            with dve.Fori(0, 3) as g:
                it = st.inside(g, 2, (0, 0))
                for b in range(2):
                    mod_evac(it, 2 * g + 2 + b, b)
            st.passed(3, 2, (0, 0))
            mod_out(dve, 7, 1)
            all_read(dve, (4, 4))
            for v in range(2):
                last = nc.vector.scalar_tensor_tensor(mpre[:, v, 1, :], mpre[:, v, 1, :], 1.0,
                                                      pcol("norm1_g", 0, KT), ALU.add, ALU.mult)
            last.then_inc(S["mod_a"], 1)
            apply_dve(dve, 0, 2, [job for q in range(4) for job in ((xT, 0, hh, hl, q), (ctxT, 1, ch, cl, q))])

            dve.wait_ge(S["spill_ok"], 16)
            nc.vector.memset(lrn[:, :, :, RANK:RANK + 1], 1.0)
            for n, (c0, width, cw) in enumerate(TOKEN):
                split_ahead(C, st, width=width, nwidth=NEXT_W[n])
                group_done(dve, st)
                src = acc[n % 2][:, :].rearrange("p (t n) -> p t n", t=2)
                if c0 == C_K:
                    last = nc.vector.tensor_copy(kn[:, :, :], src)
                elif c0 == C_Q:
                    last = nc.vector.tensor_scalar(qn[:, :, :], src, float(DK) ** -0.5, None, ALU.mult)
                elif c0 < C_GOUT:
                    last = nc.vector.tensor_copy(vn[:, :, c0 - C_V:c0 - C_V + GC], src)
                elif c0 == C_LR:
                    for t in range(2):
                        nc.vector.tensor_copy(lrn[:, t, :, 0:RANK],
                                              src[:, t, 0:cw].rearrange("p (d r) -> p d r", d=2))
                    last = nc.vector.tensor_copy(un[:, :, 0:GC - cw], src[:, :, cw:GC])
                else:
                    u0 = c0 - C_U
                    last = nc.vector.tensor_copy(un[:, :, u0:u0 + width], src[:, :, 0:width])
                last.then_inc(acc_free[n % 2], 1)
            dve.wait_ge(S["spill_ok"], 16)
            nc.vector.memset(sT[:, :, :], 0.0).then_inc(S["nat_v"], 4)
            ticks = Ticks()
            tick = lambda count: mod_ticks_dve(dve, st, ticks, count)
            for m, (src, d, t) in enumerate(SCANS):
                l = m - 4
                dve.wait_ge(S["lrT_ps"], m + 1)
                nc.vector.tensor_copy(lrT[:, :], mp[0][0:RANK + 1, 0:P]).then_inc(S["lrT_sb"], 1)
                tick(T_LR)
                dve.wait_ge(S["ln_ok"], m + 1)
                nc.vector.scalar_tensor_tensor(lab[:, m % 2, :], mp[0][:, GC:2 * GC], 0.0, tq[:, 0, :],
                                               ALU.min, ALU.subtract).then_inc(S["la_ok"], 1)
                tick(T_Z[src])
                dve.wait_ge(S["kexp_ok"], m + 1)
                nc.vector.tensor_tensor(keb[:, m % 2, :], (kn if src else ckn)[:, t, :], tq[:, 1, :],
                                        ALU.mult).then_inc(S["ke_ok"], 1)
                if src:
                    dve.wait_ge(S["qexp_ok"], l + 1)
                    nc.vector.tensor_tensor(tmp[:, 1, 0:GC], qn[:, t, :], tmp[:, 0, 0:GC], ALU.mult)
                    nc.vector.tensor_tensor(tmp[:, 1, GC:2 * GC], kn[:, t, :], tmp[:, 0, GC:2 * GC],
                                            ALU.mult).then_inc(S["qk_ok"], 1)
                tick(T_CUM[src])
                if src:
                    dve.wait_ge(S["qkT_ps"], l + 1)
                    nc.vector.tensor_copy(qdT[:, :], mp[0][:, 0:GC]).then_inc(S["qkT_sb"], 1)
                    tick(T_QK)
                    dve.wait_ge(S["sc_ps"], l + 1)
                    nc.vector.copy_predicated(
                        sT[:, d, :].rearrange("p (h n) -> p h n", h=HEADS),
                        cum_w[d].bitcast(u32).rearrange("p (a n) -> p a n", a=1).to_broadcast([P, HEADS, P]),
                        mp[1][:, 0:GC].rearrange("p (h n) -> p h n", h=HEADS)).then_inc(S["sc_sb"], 1)
                    tick(T_SC)
                for ci in range(2):
                    dve.wait_ge(S["u_ps"], 2 * m + ci + 1)
                    if src and t == (1, 0)[d] and ci == 1:
                        tick(T_STATE)
                        break
                    half = (ci, 1 - ci)[d]
                    if not src and t == (0, 1)[d] and ci == 0:
                        nc.vector.tensor_copy(state[:, d, :, :].rearrange("p h n -> p (h n)"), mp[1][:, :])\
                            .then_inc(S["st_ok"], 1)
                        tick(T_STATE)
                        continue
                    for h in range(HEADS):
                        last = nc.vector.scalar_tensor_tensor(
                            state[:, d, h, :], state[:, d, h, :], dec[:, h, half:half + 1],
                            mp[1][:, h * DV:(h + 1) * DV], ALU.mult, ALU.add)
                    last.then_inc(S["st_ok"], 1)
                    tick(T_STATE)
                if src:
                    if d == 0:
                        nc.vector.tensor_copy(osb[:, t, :], mp[0][:, :]).then_inc(S["o_ok"], 1)
                    else:
                        nc.vector.tensor_tensor(osb[:, t, :], mp[0][:, :], osb[:, t, :], ALU.add)\
                            .then_inc(S["o_ok"], 1)
            tick(T_ONORM)
            dve.wait_ge(S["ort_ok"], 1)
            own(nc.vector.reciprocal(oss[:, 0, :], oss[:, 1, :]))
            for t in range(2):
                for h in range(HEADS):
                    n = t * HEADS + h
                    part = osb[:, t, h * DV:(h + 1) * DV]
                    last = nc.vector.tensor_scalar(part, part, oss[:, 0, n:n + 1], None, ALU.mult)
            last.then_inc(S["ons_ok"], 1)
            for g in range(FGROUPS):
                tick(T_FFT)
                dve.wait_ge(S["yhi_ok"], g + 1)
                nc.vector.tensor_tensor(yfl[:, 2 * g:2 * g + 2, :], tiles(mp[1][:, 0:2 * NT]),
                                        yfh[:, 2 * g:2 * g + 2, :].bitcast(f32), ALU.subtract)\
                    .then_inc(S["ylo_ok"], 1)
                tick(T_FFT)
            mod_row(dve, st, 0)
            mod_out(dve, 23, 0)
            for g in range(2):
                split_ahead(C, st)
                group_done(dve, st)
                i = (7 + g) % 2
                dve.wait_ge(S["sg_a"], g + 1)
                nc.vector.tensor_tensor(sg[:, 4 * g:4 * g + 4, :], tiles(acc[i][:, :]),
                                        sg[:, 4 * g:4 * g + 4, :], ALU.mult).then_inc(S["sg_v"], 1)
            dve.wait_ge(S["sg_v"], 2)
            for q in range(2):
                dve.wait_ge(S["oT_ps"], q + 1)
                for t in range(4):
                    i = 4 * q + t
                    last = nc.vector.scalar_tensor_tensor(
                        tmp[:, q, t * NT:(t + 1) * NT], mp[q][:, t * NT:(t + 1) * NT],
                        pcol("gla_norm_g", i % 2), sg[:, i, :], ALU.mult, ALU.mult)
                last.then_inc(S["ot_ok"], 1)
            for q in range(2):
                dve.wait_ge(S["ohi_ok"], q + 1)
                nc.vector.tensor_tensor(ol[:, 4 * q:4 * q + 4, :], tiles(tmp[:, q, :]),
                                        oh[:, 4 * q:4 * q + 4, :].bitcast(f32), ALU.subtract)\
                    .then_inc(S["olo_ok"], 1)

            all_read(dve, F_MOD)
            with dve.Fori(0, 4) as j:
                it = st.inside(j, 3, (0, 0))
                for _ in range(2):
                    split_ahead(C, it)
                C(it, (2, 3))
                for i in range(2):
                    dve.wait_ge(used[2 * i + 1], 2 * it.u[2 * i + 1])
                    dve.wait_ge(S["gate_ok"], 2 * j + 1 + i)
                    nc.vector.tensor_tensor(tmp[:, i, :], acc[1 - i][:, :], tmp[:, i, :], ALU.mult)\
                        .then_inc(S["mrg_ok"], 1)
                    if i == 0:
                        C(it, (0, 1))
                dve.wait_ge(S["mrg_ok"], 2 * j + 2 + 2)
                nc.vector.tensor_tensor(tmp[:, 0, :], tmp[:, 0, :], tmp[:, 1, :], ALU.add)\
                    .then_inc(S["mt_ok"], 1)
                dve.wait_ge(S["mhi_ok"], j + 1)
                nc.vector.tensor_tensor(ml[:, ds(4 * j, 4), :], tiles(tmp[:, 0, :]),
                                        mh[:, ds(4 * j, 4), :].bitcast(f32), ALU.subtract)\
                    .then_inc(S["mlo_ok"], 1)
            st.passed(4, 3, (0, 0))

            def add_scaled(i, base, gate):
                for t in range(4):
                    x = xT2[:, ds(base + t, 1), :].rearrange("p a n -> p (a n)")
                    last = nc.vector.scalar_tensor_tensor(x, acc[i][:, t * NT:(t + 1) * NT],
                                                          mods[:, ds(gate + base + t, 1)], x,
                                                          ALU.mult, ALU.add)
                return last
            dve.wait_ge(S["x_back"], 16)
            with dve.Fori(0, 2) as g:
                it = st.inside(g, 2, (0, 0))
                for b in range(2):
                    split_ahead(C, it)
                    group_done(dve, it)
                    add_scaled(1 - b, 8 * g + 4 * b, 0).then_inc(acc_free[1 - b], 1)
            st.passed(2, 2, (0, 0))
            nc.vector.scalar_tensor_tensor(a2[:, :], mods[:, 2 * KT:3 * KT], 1.0, pcol("norm2_g", 0, KT),
                                           ALU.add, ALU.mult).then_inc(S["mod_b"], 1)
            norm_rstd(dve, 2)
            apply_dve(dve, 8, 3, [(xT2, 2, hh, hl, q) for q in range(4)])
            with dve.Fori(0, MLP_CHUNKS) as c:
                it = st.inside(c, 8, (0, 0))
                for g in range(4):
                    n = 4 * c + g
                    split_ahead(C, it)
                    group_done(dve, it)
                    dve.wait_ge(S["relu_ok"], n + 1)
                    nc.vector.scalar_tensor_tensor(tmp[:, 1, :], acc[g % 2][:, :], 0.0, tmp[:, 0, :],
                                                   ALU.max, ALU.mult).then_inc(S["rsq_ok"], 1)
                    dve.wait_ge(S["hhi_ok"], n + 1)
                    nc.vector.tensor_tensor(ml[:, 4 * g:4 * g + 4, :], tiles(tmp[:, 1, :]),
                                            mh[:, 4 * g:4 * g + 4, :].bitcast(f32), ALU.subtract)\
                        .then_inc(S["hid_ok"], 1)
                for g in range(4):
                    split_ahead(C, it)
                    group_done(dve, it)
                    add_scaled(g % 2, 4 * g, 3 * KT).then_inc(acc_free[g % 2], 1)
            st.passed(MLP_CHUNKS, 8, (0, 0))
            norm_rstd(dve, 3)
            dve.wait_ge(S["rs_ok"], 4)
            dve.wait_ge(S["ms_ok"], 16)
            for q in range(4):
                own(nc.vector.tensor_tensor(tiles(tmp[:, q % 2, :]), xT2[:, 4 * q:4 * q + 4, :], rbc(3),
                                            ALU.mult))
                for t in range(4):
                    last = nc.vector.tensor_scalar(xT2[:, 4 * q + t, :], tmp[:, q % 2, t * NT:(t + 1) * NT],
                                                   pcol("final_norm_g", 4 * q + t), None, ALU.mult)
                last.then_inc(S["vt_ok"], 1)
            norm_rstd(dve, 4)
            apply_dve(dve, 12, 5, [(xT2, 4, hh, hl, q) for q in range(4)])
            with dve.Fori(0, 2) as g:
                it = st.inside(g, 2, (0, 0))
                for b in range(2):
                    split_ahead(C, it)
                    group_done(dve, it)
                    nc.vector.tensor_copy(uT[:, ds(3 * TA + 8 * g + 4 * b, 4), :], tiles(acc[b][:, :]))\
                        .then_inc(acc_free[b], 1)
            st.passed(2, 2, (0, 0))
            dve.wait_ge(S["bsig_ok"], 1)
            own(nc.vector.tensor_tensor(uT[:, 18:24, :], uT[:, 18:24, :], uT[:, 24:30, :], ALU.mult))

            def tap(i, sh):
                def tile(t):
                    return uT[:, ds(t + i, 1), :].rearrange("p a n -> p (a n)")
                x, done = tile(18), (KCONV + 1) * i
                if sh == KCONV:
                    dve.wait_ge(S["tap_ok"], done + KCONV + 1)
                    ins = nc.vector.tensor_tensor(tile(24), cacc[:, 0, :], cacc[:, 1, :], ALU.add)
                else:
                    dve.wait_ge(S["tap_ok"], done + max(sh, 1))
                    w = par[:, ds(COL["conv_b_w_2"] + TB * (KCONV - 1 - sh) + i, 1)]
                    part = cacc[:, sh % 2, sh:NT]
                    if sh == 0:
                        ins = nc.vector.tensor_scalar(part, x, w, par[:, ds(COL["conv_b_bias_2"] + i, 1)],
                                                      ALU.mult, ALU.add)
                    elif sh == 1:
                        nc.vector.memset(cacc[:, 1, 0:1], 0.0)
                        ins = nc.vector.tensor_scalar(part, x[:, 0:NT - 1], w, None, ALU.mult)
                    else:
                        ins = nc.vector.scalar_tensor_tensor(part, x[:, 0:NT - sh], w, part, ALU.mult, ALU.add)
                ins.then_inc(S["tap_ok"], 1)

            def taps(g, n0):
                piece = [0]

                def add():
                    for n in range(n0 + 6 * piece[0], n0 + 6 * piece[0] + 6):
                        tap(3 * g + n // (KCONV + 1), n % (KCONV + 1))
                    piece[0] += 1
                return add
            with dve.Fori(0, 2) as g:
                it = st.inside(g, 2, (0, 0))
                for b in range(2):
                    split_ahead(C, it, behind=taps(g, 48 * b))
                    group_done(dve, it)
                    nc.vector.tensor_copy(uT[:, ds(8 * g + 4 * b, 4), :], tiles(acc[b][:, :]))\
                        .then_inc(acc_free[b], 1)
            st.passed(2, 2, (0, 0))
            split_ahead(C, st, width=C2_B - 4 * GC)
            group_done(dve, st)
            nc.vector.tensor_copy(uT[:, 16:18, :], tiles(acc[0][:, 0:2 * NT]))\
                .then_inc(acc_free[0], 1)
            all_read(dve, F_U)
            own(nc.vector.tensor_tensor(uT[:, 6:12, :], uT[:, 6:12, :], uT[:, 12:18, :], ALU.mult))
            for sh in range(3):
                for t in range(TA):
                    w = pcol("conv_a_w_2", TA * (2 - sh) + t)
                    x, y = uT[:, 6 + t, 0:NT - sh], uT[:, 12 + t, sh:NT]
                    if sh == 0:
                        last = nc.vector.tensor_scalar(y, x, w, None, ALU.mult)
                    else:
                        last = nc.vector.scalar_tensor_tensor(y, x, w, y, ALU.mult, ALU.add)
                own(last)
            nc.vector.tensor_tensor(uT[:, 12:18, :], uT[:, 12:18, :], uT[:, 0:6, :], ALU.mult)\
                .then_inc(S["a_ok"], 1)
            dve.wait_ge(S["ln_ps"], 1)
            own(nc.vector.tensor_scalar(root[:, :], mp[1][:, 0:NT], 1.0 / WB, None, ALU.mult))
            nc.vector.tensor_tensor(uT[:, 24:30, :], uT[:, 24:30, :],
                                    root[:, :].rearrange("p (a n) -> p a n", a=1).to_broadcast([P, TB, NT]),
                                    ALU.subtract).then_inc(S["ln_d"], 1)
            pa, pb = tiles(tmp[:, 0, :]), tiles(tmp[:, 1, :])
            src, dst = uT[:, 30:34, :], pa
            for g in range(TC):
                sh = 1 << g
                nc.vector.tensor_copy(dst[:, g:4, 0:sh], src[:, g:4, 0:sh])
                own(nc.vector.tensor_tensor(dst[:, g:4, sh:NT], src[:, g:4, sh:NT], src[:, g:4, 0:NT - sh],
                                            ALU.add))
                part = dst[:, g, :]
                own(nc.vector.tensor_tensor(part[:, 0:16], part[:, 0:16], fix_w[:, g, :], ALU.mult)
                    if g == 3 else
                    nc.vector.tensor_tensor(fixed[:, g, :], part[:, 0:16], fix_w[:, g, :], ALU.mult))
                src, dst = dst, (pb, pa)[(g + 1) % 2 == 0]
            for g in range(TC):
                w = 2 << g
                part = (pa, pb)[g % 2][:, g, :]
                x = uT[:, 30 + g, :]
                if g < 3:
                    nc.vector.scalar_tensor_tensor(x[:, 0:16], fixed[:, g, :], 1.0 / w, x[:, 0:16],
                                                   ALU.mult, ALU.subtract)
                    last = nc.vector.scalar_tensor_tensor(x[:, 16:NT], part[:, 16:NT], 1.0 / w, x[:, 16:NT],
                                                          ALU.mult, ALU.subtract)
                else:
                    last = nc.vector.scalar_tensor_tensor(x, part, 1.0 / w, x, ALU.mult, ALU.subtract)
            last.then_inc(S["pooled_ok"], 1)
            dve.wait_ge(S["mxh_ok"], 1)
            nc.vector.tensor_tensor(ml[:, 0:TA, :], uT[:, 12:18, :], mh[:, 0:TA, :].bitcast(f32),
                                    ALU.subtract).then_inc(S["mxl_ok"], 1)
            dve.wait_ge(S["mxh_ok"], 2)
            nc.vector.tensor_tensor(ml[:, 12:16, :], uT[:, 30:34, :], mh[:, 12:16, :].bitcast(f32),
                                    ALU.subtract).then_inc(S["mxl_ok"], 1)
            dve.wait_ge(S["ln_rt"], 1)
            own(nc.vector.reciprocal(rstd[:, 1, :], root[:, :]))
            nc.vector.tensor_tensor(uT[:, 24:30, :], uT[:, 24:30, :], rbc(1, TB), ALU.mult)\
                .then_inc(S["ln_d"], 1)
            dve.wait_ge(S["ln_sg"], 1)
            nc.vector.tensor_tensor(uT[:, 24:30, :], uT[:, 24:30, :],
                                    tmp[:, :, :].rearrange("p a n -> p (a n)")[:, 0:2 * WB]
                                    .rearrange("p (t n) -> p t n", n=NT), ALU.mult).then_inc(S["ln_d"], 1)
            dve.wait_ge(S["mxh_ok"], 3)
            nc.vector.tensor_tensor(ml[:, 6:12, :], uT[:, 24:30, :], mh[:, 6:12, :].bitcast(f32),
                                    ALU.subtract).then_inc(S["mxl_ok"], 1)
            with dve.Fori(0, 2) as g:
                it = st.inside(g, 2, (0, 0))
                for b in range(2):
                    split_ahead(C, it)
                    group_done(dve, it)
                    nc.vector.tensor_copy(yT[:, ds(8 * g + 4 * b, 4), :], tiles(acc[1 - b][:, :]))\
                        .then_inc(acc_free[1 - b], 1)
            st.passed(2, 2, (0, 0))

            def norm_add(k, name, sem_ok):
                norm_rstd(dve, k)
                dve.wait_ge(S["rs_ok"], k + 1)
                for q in range(4):
                    own(nc.vector.tensor_tensor(tiles(tmp[:, q % 2, :]), yT[:, 4 * q:4 * q + 4, :], rbc(k),
                                                ALU.mult))
                    for t in range(4):
                        x = xT2[:, 4 * q + t, :]
                        last = nc.vector.scalar_tensor_tensor(x, tmp[:, q % 2, t * NT:(t + 1) * NT],
                                                              pcol(name, 4 * q + t), x, ALU.mult, ALU.add)
                    last.then_inc(sem_ok, 1)
            norm_add(5, "norm_mix_post_2", S["vt_ok"])
            own(nc.vector.memset(yT[:, :, :], 0.0))
            norm_rstd(dve, 6)
            apply_dve(dve, 16, 7, [(xT2, 6, hh, hl, q) for q in range(4)])

            def ffn_pair(it, c, p, n):
                for v in range(2):
                    split_ahead(C, it)
                    group_done(dve, it)
                    up = (up1, up2)[v]
                    dve.wait_ge(S["ct_ok"], 2 * n + v + 1)
                    for sh in (1, 2):
                        for t in range(4):
                            col = COL["conv_ffn_w_2"] + 2 * FT * (2 - sh) + 16 * c + 4 * p + t + FT * v
                            y = up[:, t, sh:NT]
                            last = nc.vector.scalar_tensor_tensor(
                                y, acc[v][:, t * NT:(t + 1) * NT - sh], par[:, ds(col, 1)], y,
                                ALU.mult, ALU.add)
                        if sh == 1:
                            last.then_inc(S["tap2_ok"], 1)
                            dve.wait_ge(S["tap2_ok"], 2 * n + v + 1)
                    last.then_inc(S["cd_ok"], 1)
                    if v == 0:
                        dve.wait_ge(S["gs_ok"], n + 1)
                        nc.vector.tensor_tensor(up1[:, :, :], up1[:, :, :], tiles(tmp[:, 0, :]), ALU.mult)\
                            .then_inc(S["gu_ok"], 1)
                    else:
                        dve.wait_ge(S["gu_ok"], n + 1)
                        dve.wait_ge(S["cd_ok"], 2 * n + 2)
                        nc.vector.tensor_tensor(tiles(tmp[:, 1, :]), up1[:, :, :], up2[:, :, :], ALU.mult)\
                            .then_inc(S["gm_ok"], 1)
                        dve.wait_ge(S["fhi_ok"], n + 1)
                        nc.vector.tensor_tensor(ml[:, 4 * p:4 * p + 4, :], tiles(tmp[:, 1, :]),
                                                mh[:, 4 * p:4 * p + 4, :].bitcast(f32), ALU.subtract)\
                            .then_inc(S["fid_ok"], 1)

            def down_add(g, n):
                y = yT[:, 4 * g:4 * g + 4, :]
                nc.vector.tensor_tensor(y, tiles(acc[g % 2][:, :]), y, ALU.add)\
                    .then_inc(acc_free[g % 2], 1)
            with dve.Fori(0, 2) as c:
                it = st.inside(c, 12, (0, 0))
                for p in range(4):
                    ffn_pair(it, c, p, 4 * c + p)
                for g in range(4):
                    split_ahead(C, it)
                    group_done(dve, it)
                    down_add(g, 4 * c + g)
            st.passed(2, 12, (0, 0))
            for p in range(3):
                ffn_pair(st, 2, p, 8 + p)
            for g in range(4):
                split_ahead(C, st, slots=3, last=g == 3)
                group_done(dve, st, slots=3)
                down_add(g, 8 + g)
            all_read(dve, F_FFN)
            norm_add(7, "norm_ffn_post_2", S["vt_ok"])
            for q in range(4):
                dve.wait_ge(S["out_ps"], q + 1)
                nc.vector.tensor_copy(outn[:, :, 4 * q * P:(4 * q + 4) * P],
                                      mp[q % 2][:, :].rearrange("p (t n) -> p t n", t=2))\
                    .then_inc(S["out_sb"], 1)

        @block.tensor
        def _(pe):
            st = Turns()
            pe.wait_ge(S["con_in"], 16)
            pe.wait_ge(S["par_in"], 16 * NPDMA)
            rows = tmp[:, 0, 0:NPB * P].rearrange("p (b n) -> p b n", b=NPB)
            for b in range(NPB):
                n = min(P, NPARAM - b * P)
                last = nc.tensor.transpose(mp[1][:, b * P:b * P + n], rows[0:n, b, :], ident[0:n, 0:n])
            last.then_inc(S["par_ps"], 1)

            def mm_mod(it, n, i):
                for s in range(4):
                    for j in range(2):
                        mod_piece(pe, it, i, s, j)
                    if s == 1 and not (isinstance(n, int) and n == 0):
                        mod_turn(pe, n - 1, 1 - i)
            pe.wait_ge(S["cv_ok"], 1)
            for g in range(2):
                mm_mod(st, g, g)
            for n in range(8):
                q = n % 4
                if n == 0:
                    pe.wait_ge(S["x_in"], 32)
                    pe.wait_ge(S["par_sb"], 1)
                if n == 4:
                    pe.wait_ge(S["ctx_in"], 16)
                if n >= 2:
                    pe.wait_ge(S["xt_sb"], min(n - 1, 4))
                if n >= 6:
                    pe.wait_ge(S["ct_sb"], n - 5)
                src = stage_c if n >= 4 else stage_x
                for f in range(4):
                    for t in range(2):
                        last = nc.tensor.transpose(mp[n % 2][:, f * NT + t * P:f * NT + (t + 1) * P],
                                                   src[:, t, (4 * q + f) * P:(4 * q + f + 1) * P], ident)
                last.then_inc(S["xt_ps"], 1)
            pe.wait_ge(S["eps_ok"], 3)
            pe.wait_ge(S["ct_sb"], 4)
            norm_sums(pe, 0, mp[0])
            norm_sums(pe, 1, mp[1])
            with pe.Fori(0, 3) as g:
                it = st.inside(g, 2, (1, 1))
                for b in range(2):
                    mm_mod(it, 2 * g + 2 + b, b)
            st.passed(3, 2, (1, 1))
            mod_turn(pe, 7, 1)
            for n, (c0, width, cw) in enumerate(TOKEN):
                mm_token(pe, st, n % 2, width, cw, ready=h_ready(pe, 0, 2) if n == 0 else None)
            pe.wait_ge(S["gla_in"], 80)
            pe.wait_ge(S["nat_v"], 4)
            pe.wait_ge(acc_free[1], st.f[1])
            pe.wait_ge(acc_free[0], st.f[0])
            stc = 0
            ticks = Ticks()
            tick = lambda count: mod_ticks_pe(pe, st, ticks, count)
            for m, (src, d, t) in enumerate(SCANS):
                l = m - 4
                if m >= 5:
                    pe.wait_ge(S["o_ok"], l)
                elif m:
                    pe.wait_ge(S["kexp_ok"], m)
                nc.tensor.transpose(mp[0][0:RANK + 1, 0:P], lrn[:, (t if src else 2 + t), d, 0:RANK + 1], ident)\
                    .then_inc(S["lrT_ps"], 1)
                tick(T_LR)
                pe.wait_ge(S["lrT_sb"], m + 1)
                nc.tensor.matmul(mp[0][:, GC:2 * GC], lrT[:, :], wlr[:, d, :], start=True, stop=True)\
                    .then_inc(S["z_ps"], 1)
                tick(T_Z[src])
                pe.wait_ge(S["la_ok"], m + 1)
                if stc:
                    pe.wait_ge(S["st_ok"], stc)
                la = lab[:, m % 2, :]
                nc.tensor.matmul(mp[1][:, 0:GC], end_w[d], la, start=True, stop=True)
                if src:
                    nc.tensor.matmul(mp[1][:, GC:2 * GC], cum_w[d], la, start=True, stop=True)
                for h in range(HEADS):
                    last = nc.tensor.matmul(mp[0][:, 2 * h:2 * h + 2], la[:, h * DK:(h + 1) * DK], half_w,
                                            start=True, stop=True)
                last.then_inc(S["cum_ps"], 1)
                tick(T_CUM[src])
                pe.wait_ge(S["ke_ok"], m + 1)
                v = vn if src else cvn
                if src:
                    pe.wait_ge(S["qk_ok"], l + 1)
                    for x in range(2):
                        for h in range(HEADS):
                            last = nc.tensor.transpose(mp[0][:, x * GC + h * P:x * GC + (h + 1) * P],
                                                       tmp[:, 1, x * GC + h * P:x * GC + (h + 1) * P], ident)
                    last.then_inc(S["qkT_ps"], 1)
                    tick(T_QK)
                    pe.wait_ge(S["qkT_sb"], 2 * l + 2)
                    for h in range(HEADS):
                        cols = slice(h * P, (h + 1) * P)
                        last = nc.tensor.matmul(mp[1][:, cols], kiT[:, cols], qdT[:, cols],
                                                start=True, stop=True)
                    last.then_inc(S["sc_ps"], 1)
                    tick(T_SC)
                    pe.wait_ge(S["sc_sb"], l + 1)
                    for h in range(HEADS):
                        nc.tensor.matmul(mp[0][:, h * DV:(h + 1) * DV], sT[:, d, h * P:(h + 1) * P],
                                         v[:, t, h * DV:(h + 1) * DV], start=h % 2 == 0, stop=False,
                                         skip_group_check=True)
                for ci in range(2):
                    half = (ci, 1 - ci)[d]
                    rows = slice(half * CHUNK, (half + 1) * CHUNK)
                    if stc:
                        pe.wait_ge(S["st_ok"], stc)
                    if src:
                        for h in range(HEADS):
                            last = nc.tensor.matmul(mp[0][rows, h * DV:(h + 1) * DV],
                                                    qdT[:, h * P + half * CHUNK:h * P + (half + 1) * CHUNK],
                                                    state[:, d, h, :], start=False, stop=True,
                                                    skip_group_check=True)
                    if not (src and t == (1, 0)[d] and ci == 1):
                        for h in range(HEADS):
                            last = nc.tensor.matmul(mp[1][:, h * DV:(h + 1) * DV],
                                                    keb[rows, m % 2, h * DK:(h + 1) * DK],
                                                    v[rows, t, h * DV:(h + 1) * DV], start=h % 2 == 0,
                                                    stop=True, skip_group_check=True)
                        stc += 1
                    last.then_inc(S["u_ps"], 1)
                    tick(T_STATE)
            tick(T_ONORM)
            pe.wait_ge(S["dft_in"], 16)
            for g in range(FGROUPS):
                if g:
                    pe.wait_ge(S["p_sb"], g)
                else:
                    pe.wait_ge(S["o_ok"], 4)
                for dt in range(2):
                    c0 = g * FDIM + dt * P
                    for t in range(2):
                        last = nc.tensor.matmul(mp[0][:, dt * GC:(dt + 1) * GC], un[:, t, c0:c0 + P],
                                                dft[:, t, :], start=t == 0, stop=t == 1)
                last.then_inc(S["p_ps"], 1)
                tick(T_FFT)
                pe.wait_ge(S["p_sb"], g + 1)
                if g:
                    pe.wait_ge(S["ylo_ok"], g)
                for dt in range(2):
                    for part in range(2):
                        for t in range(2):
                            c0 = part * NT + dt * P
                            last = nc.tensor.matmul(mp[1][:, dt * NT:(dt + 1) * NT], dft[:, t, c0:c0 + P],
                                                    pbuf[:, t, part * NT:(part + 1) * NT],
                                                    start=part + t == 0, stop=part + t == 2)
                last.then_inc(S["y_ps"], 1)
                tick(T_FFT)
            mod_turn(pe, 23, 0)
            for g in range(2):
                mm_feature(pe, st, (7 + g) % 2, hh, hl, 0)
            pe.wait_ge(S["ons_ok"], 1)
            pe.wait_ge(S["ylo_ok"], 4)
            for q in range(2):
                for f in range(4):
                    for t in range(2):
                        c0 = (4 * q + f) * P
                        last = nc.tensor.transpose(mp[q][:, f * NT + t * P:f * NT + (t + 1) * P],
                                                   osb[:, t, c0:c0 + P], ident)
                last.then_inc(S["oT_ps"], 1)

            pe.wait_ge(S["olo_ok"], 2)
            with pe.Fori(0, 4) as j:
                it = st.inside(j, 3, (0, 0))
                for i in range(2):
                    pe.wait_ge(S["sg_v"], 2)
                    mm_feature(pe, it, 1 - i, hh, hl, 0, free=(S["mrg_ok"], 2 * j + 1 + i))
                mm_feature(pe, it, 1, yfh, yfl, 0, which=(0, 1), free=(S["gate_ok"], 2 * j + 1))
                mm_feature(pe, it, 0, oh, ol, 0, which=(2, 3), free=(S["gate_ok"], 2 * j + 2))
            st.passed(4, 3, (0, 0))

            pe.wait_ge(S["mrg_ok"], 2 + 8)

            def merged(s):
                pe.wait_ge(S["mlo_ok"], s + 2)
            with pe.Fori(0, 2) as g:
                it = st.inside(g, 2, (1, 1))
                for b in range(2):
                    mm_feature(pe, it, 1 - b, mh, ml, 1, ready=merged)
            st.passed(2, 2, (1, 1))
            norm_sums(pe, 2, mp[0])
            with pe.Fori(0, MLP_CHUNKS) as c:
                it = st.inside(c, 8, (2, 2))
                for g in range(4):
                    mm_feature(pe, it, g % 2, hh, hl, 0, ready=h_ready(pe, 8),
                               free=(S["rsq_ok"], 4 * c + g - 1) if g >= 2 else None)
                for g in range(4):
                    mm_feature(pe, it, g % 2, mh, ml, 1, free=(S["rsq_ok"], 4 * c + g + 3) if g < 2 else None,
                               ready=(lambda s: pe.wait_ge(S["hid_ok"], 4 * c + s + 1)) if g == 0 else None)
            st.passed(MLP_CHUNKS, 8, (2, 2))
            norm_sums(pe, 3, mp[0])
            pe.wait_ge(S["rt_ok"], 4)
            norm_sums(pe, 4, mp[0])
            with pe.Fori(0, 4) as g:
                it = st.inside(g, 2, (1, 1))
                for b in range(2):
                    mm_feature(pe, it, b, hh, hl, 1, ready=h_ready(pe, 12))
            st.passed(4, 2, (1, 1))
            mm_feature(pe, st, 0, hh, hl, 1, ntile=2)
            pe.wait_ge(S["tap_ok"], (KCONV + 1) * TB + 1)
            for t in range(TB):
                last = nc.tensor.matmul(mp[1][:, 0:NT], ones[:, :], uT[:, 24 + t, :], start=t == 0,
                                        stop=t == TB - 1)
            last.then_inc(S["ln_ps"], 1)
            pe.wait_ge(S["pooled_ok"], 1)
            pe.wait_ge(S["pw_in"], 16)
            pe.wait_ge(S["rt_ok"], 5)
            for t in range(TC):
                last = nc.tensor.matmul(mp[0][:, t * NT:(t + 1) * NT], pw[:, t, :], uT[:, 30 + t, :],
                                        start=True, stop=True)
            last.then_inc(S["pool_ps"], 1)
            pe.wait_ge(S["ln_sq"], 1)
            for t in range(TB):
                last = nc.tensor.matmul(mp[1][:, GC:GC + NT], ones[:, :],
                                        tmp[:, t // 4, (t % 4) * NT:(t % 4 + 1) * NT], start=t == 0,
                                        stop=t == TB - 1)
            last.then_inc(S["ln_ps"], 1)
            pe.wait_ge(S["mxl_ok"], 3)
            with pe.Fori(0, 2) as g:
                it = st.inside(g, 2, (1, 1))
                for b in range(2):
                    mm_feature(pe, it, 1 - b, mh, ml, 1)
            st.passed(2, 2, (1, 1))
            norm_sums(pe, 5, mp[0])
            pe.wait_ge(S["rt_ok"], 6)
            norm_sums(pe, 6, mp[0])

            def ffn(it, c, pairs, slots):
                for p in range(pairs):
                    for v in range(2):
                        mm_feature(pe, it, v, hh, hl, 0, ready=h_ready(pe, 16),
                                   free=(S["cd_ok"], 2 * (4 * c + p) - 1 + v) if p else None)
                for g in range(4):
                    mm_feature(pe, it, g % 2, mh, ml, 1, slots=slots,
                               free=(S["cd_ok"], 2 * (4 * c + pairs) - 1 + g) if g < 2 else None,
                               ready=(lambda s: pe.wait_ge(S["fid_ok"], 4 * c + s + 1)) if g == 0 else None)
            with pe.Fori(0, 2) as c:
                ffn(st.inside(c, 12, (2, 2)), c, 4, 4)
            st.passed(2, 12, (2, 2))
            ffn(st, 2, 3, 3)
            norm_sums(pe, 7, mp[0])
            for q in range(4):
                pe.wait_ge(S["vt_ok"], 8 + q + 1)
                if q >= 2:
                    pe.wait_ge(S["out_sb"], q - 1)
                elif q == 0:
                    pe.wait_ge(S["rt_ok"], 8)
                for t in range(2):
                    for f in range(4):
                        last = nc.tensor.transpose(mp[q % 2][:, t * GC + f * P:t * GC + (f + 1) * P],
                                                   xT2[:, 4 * q + f, t * P:(t + 1) * P], ident)
                last.then_inc(S["out_ps"], 1)


def constants():
    import numpy as np
    t = np.arange(P)
    same = (t[:, None] // CHUNK) == (t[None, :] // CHUNK)
    s, q = t[:, None], t[None, :]
    tau = np.float32(1 / 16)
    con = np.zeros((P, NCON), np.float32)
    con[0:4, P + 64:P + 66] = np.eye(2)[[0, 1, 0, 1]]
    con[:, 0:P] = np.eye(P)
    con2 = np.zeros((P, 4 * P + 2), np.float32)
    for n, m in enumerate((s <= q, s >= q, s > q, s < q)):
        con2[:, n * P:(1 + n) * P] = (m & same) * tau
    con2[:, 4 * P:4 * P + 2] = (t[:, None] // CHUNK == np.arange(2)) * tau
    for g in range(4):
        w = 2 << g
        con[:, P + 16 * g:P + 16 * (g + 1)] = w / np.minimum(np.arange(16) + 1.0, w)
    n = np.arange(NT, dtype=np.float64)
    a = 2 * np.pi * ((n[:, None] * n[None, :]) % NT) / NT
    dft = (np.concatenate([np.cos(a), np.sin(a)], 1) / 16).astype(np.float32)
    quarter = D // 4
    omega = np.float32(1) / (np.float32(10000.0) ** (np.arange(quarter, dtype=np.float32) / np.float32(quarter)))
    row = np.repeat(np.arange(NT // 64, dtype=np.float32), 64)
    col = np.tile(np.arange(64, dtype=np.float32), NT // 64)
    er, ec = row[:, None] * omega, col[:, None] * omega
    pos = np.concatenate([np.sin(er), np.cos(er), np.sin(ec), np.cos(ec)], -1).astype(np.float32)
    pos = np.ascontiguousarray(pos.T.reshape(KT, P, NT).transpose(1, 0, 2)).reshape(P, KT * NT)
    return {"con": con, "con2": con2, "dft": dft, "posT": pos}


WEIGHTS = ["w_mod", "w_in", "w_lr_f", "w_lr_b", "w_fourier_out", "w_gla_out", "w_out", "w_mlp_in",
           "w_mlp_out", "w_in_2", "w_out_2", "w_up_2", "w_down_2"]


def kernel(**inputs):
    import numpy as np
    import concourse.bacc as bacc
    from concourse.bass_utils import run_bass_kernel_spmd as run

    x = {k: np.ascontiguousarray(v) for k, v in inputs.items()}
    arrays = dict(constants())
    arrays["x"], arrays["ctx"] = x["x"].reshape(NT, D), x["ctx"].reshape(NT, D)
    for name in WEIGHTS:
        arrays[name] = x[name].reshape(x[name].shape[1:])
    arrays["pool_w_2"] = x["pool_w_2"].reshape(TC * P, P)
    for name in ("b_lr_f", "b_lr_b"):
        arrays[name] = x[name].reshape(1, KEYW)
    for name, n in PROWS:
        arrays[name] = x[name].reshape(n, P)
    nc = bacc.Bacc("TRN2", target_bir_lowering=False, num_devices=1)
    ins = {k: nc.dram_tensor(f"in_{k}", a.shape, mybir.dt.from_np(a.dtype), kind="ExternalInput").ap()
           for k, a in arrays.items()}
    out = nc.dram_tensor("out", (NT, D), mybir.dt.float32, kind="ExternalOutput").ap()
    build(nc, ins, out)
    r = run(nc, [{f"in_{k}": a for k, a in arrays.items()}], core_ids=[0])
    return r.results[0]["out"].reshape(1, NT, D)
```
